# Optimizing a Trainium2 kernel written in Bass

```python
import math
import jax
import jax.numpy as jnp
from jax import lax
import numpy as np

D_MODEL = 1024
BATCH = 1
SEQ = 128
DEPTH = 2
DEC_BATCH = 1
DEC_SEQ = 512
PAST_LEN = 128

GRID_W = 64
HEAD_DIM = 64
H_A = 6
NA_ROWS = 8
NA_COLS = 16
NA_QCOLS = 16
NA_KCOLS = 32
H_B = 4
DQK_B = 32
DV_B = 64
H_C = 6
KV_C = 2
MIX_WIDTH = H_A * HEAD_DIM + H_B * DV_B + H_C * HEAD_DIM
IN_SIZES = (H_A * HEAD_DIM, H_A * HEAD_DIM, H_A * HEAD_DIM,
            H_B * 2 * DQK_B, H_B * 2 * DQK_B, H_B * DV_B,
            H_C * HEAD_DIM, KV_C * HEAD_DIM, KV_C * HEAD_DIM)
IN_WIDTH = sum(IN_SIZES)
N_KEYS = 128
N_EXPERTS = N_KEYS * N_KEYS
PEER_HEADS = 8
PEER_TOPK = 16
PEER_DQ = 256
PEER_TOK_BLOCK = 128

Q_BLOCK = 128
ROPE_THETA = 10000.0
EPS = 1e-6

kernel_name = "hybrid_dit_prefix_natten_diff_gqa_peer"

def rms_norm(x, g):
    xf = x.astype(jnp.float32)
    y = xf * lax.rsqrt(jnp.mean(xf * xf, axis=-1, keepdims=True) + EPS)
    return (y * g.astype(jnp.float32)).astype(x.dtype)

def _rope_1d(x, pos):
    d = x.shape[-1]
    inv = ROPE_THETA ** (-jnp.arange(d // 2, dtype=jnp.float32) / (d // 2))
    ang = pos.astype(jnp.float32)[:, None] * inv[None, :]
    cos = jnp.cos(ang)[None, :, None, :].astype(x.dtype)
    sin = jnp.sin(ang)[None, :, None, :].astype(x.dtype)
    x1, x2 = x[..., : d // 2], x[..., d // 2:]
    return jnp.concatenate([x1 * cos - x2 * sin, x1 * sin + x2 * cos], axis=-1)

def axial_rope(x):
    t = jnp.arange(x.shape[1])
    d = x.shape[-1]
    return jnp.concatenate([_rope_1d(x[..., : d // 2], t // GRID_W),
                            _rope_1d(x[..., d // 2:], t % GRID_W)], axis=-1)

def mixer_qkv(h, w_in_l, qk_norm_l, positioned):
    B, T, _ = h.shape
    splits = np.cumsum(IN_SIZES)[:-1].tolist()
    aq, ak, av, bq, bk, bv, cq, ck, cv = jnp.split(h @ w_in_l, splits, axis=-1)
    aq = aq.reshape(B, T, H_A, HEAD_DIM)
    ak = ak.reshape(B, T, H_A, HEAD_DIM)
    av = av.reshape(B, T, H_A, HEAD_DIM)
    bq = bq.reshape(B, T, H_B, 2, DQK_B)
    bk = bk.reshape(B, T, H_B, 2, DQK_B)
    bv = bv.reshape(B, T, H_B, DV_B)
    cq = rms_norm(cq.reshape(B, T, H_C, HEAD_DIM), qk_norm_l[0])
    ck = rms_norm(ck.reshape(B, T, KV_C, HEAD_DIM), qk_norm_l[1])
    cv = cv.reshape(B, T, KV_C, HEAD_DIM)
    if positioned:
        bq = axial_rope(bq.reshape(B, T, H_B * 2, DQK_B)).reshape(B, T, H_B, 2, DQK_B)
        bk = axial_rope(bk.reshape(B, T, H_B * 2, DQK_B)).reshape(B, T, H_B, 2, DQK_B)
        cq = axial_rope(cq)
        ck = axial_rope(ck)
    return (aq, ak, av), (bq, bk, bv), (cq, ck, cv)

def gqa_attend(q, k, v):
    B, Tq, H, d = q.shape
    kv = k.shape[2]
    g = H // kv
    nb = Tq // Q_BLOCK
    qb = q.reshape(B, nb, Q_BLOCK, kv, g, d).transpose(1, 0, 2, 3, 4, 5)

    def one(qblk):
        s = jnp.einsum('bqkgd,bskd->bkgqs', qblk, k).astype(jnp.float32) * (d ** -0.5)
        p = jax.nn.softmax(s, axis=-1).astype(v.dtype)
        return jnp.einsum('bkgqs,bskd->bqkgd', p, v)

    o = lax.map(one, qb)
    return o.transpose(1, 0, 2, 3, 4, 5).reshape(B, Tq, H * d)

def diff_attend(q, k, v, lam):
    B, Tq, H, _, d = q.shape
    nb = Tq // Q_BLOCK
    qb = q.reshape(B, nb, Q_BLOCK, H, 2, d).transpose(1, 0, 2, 3, 4, 5)

    def one(qblk):
        s = jnp.einsum('bqhcd,bshcd->bhcqs', qblk, k).astype(jnp.float32) * (d ** -0.5)
        p = jax.nn.softmax(s, axis=-1)
        pd = (p[:, :, 0] - lam * p[:, :, 1]).astype(v.dtype)
        return jnp.einsum('bhqs,bshd->bqhd', pd, v)

    o = lax.map(one, qb)
    return o.transpose(1, 0, 2, 3, 4).reshape(B, Tq, H, v.shape[-1])

def neighbourhood_attend(q, k, v, k_ctx, v_ctx, rpb):
    B, T, H, d = q.shape
    rows = T // GRID_W
    wr = min(NA_ROWS, rows)
    ncb = GRID_W // NA_QCOLS
    qc = np.arange(GRID_W)
    cs = np.clip(qc - NA_COLS // 2, 0, GRID_W - NA_COLS)
    kc0 = np.clip(cs[::NA_QCOLS], 0, GRID_W - NA_KCOLS)
    kcols = kc0[:, None] + np.arange(NA_KCOLS)[None, :]
    qcols = qc.reshape(ncb, NA_QCOLS)
    cs_b = cs.reshape(ncb, NA_QCOLS)
    col_ok = (kcols[:, None, :] >= cs_b[:, :, None]) & (kcols[:, None, :] < cs_b[:, :, None] + NA_COLS)
    mask = np.broadcast_to(col_ok[:, :, None, :], (ncb, NA_QCOLS, wr, NA_KCOLS)).reshape(ncb, NA_QCOLS, wr * NA_KCOLS)
    dc_idx = np.clip(kcols[:, None, :] - qcols[:, :, None], -(NA_COLS - 1), NA_COLS - 1) + NA_COLS - 1
    qg = q.reshape(B, rows, ncb, NA_QCOLS, H, d)
    kg = k.reshape(B, rows, GRID_W, H, d)
    vg = v.reshape(B, rows, GRID_W, H, d)
    scale = d ** -0.5
    nk = wr * NA_KCOLS

    def one_row(r):
        rs = jnp.clip(r - wr // 2, 0, rows - wr)
        k_rows = lax.dynamic_slice_in_dim(kg, rs, wr, axis=1)
        v_rows = lax.dynamic_slice_in_dim(vg, rs, wr, axis=1)
        k_blk = k_rows[:, :, kcols].transpose(0, 2, 1, 3, 4, 5).reshape(B, ncb, nk, H, d)
        v_blk = v_rows[:, :, kcols].transpose(0, 2, 1, 3, 4, 5).reshape(B, ncb, nk, H, d)
        q_row = lax.dynamic_index_in_dim(qg, r, axis=1, keepdims=False)
        dr_idx = rs + jnp.arange(wr) - r + NA_ROWS - 1
        bias = rpb[:, dr_idx][:, :, dc_idx]
        bias = bias.transpose(0, 2, 3, 1, 4).reshape(H, ncb, NA_QCOLS, nk).astype(jnp.float32)
        s_lat = jnp.einsum('bnqhd,bnkhd->bhnqk', q_row, k_blk).astype(jnp.float32) * scale + bias[None]
        s_lat = jnp.where(mask[None, None], s_lat, -jnp.inf)
        s_ctx = jnp.einsum('bnqhd,bshd->bhnqs', q_row, k_ctx).astype(jnp.float32) * scale
        p = jax.nn.softmax(jnp.concatenate([s_lat, s_ctx], axis=-1), axis=-1).astype(v.dtype)
        o = (jnp.einsum('bhnqk,bnkhd->bnqhd', p[..., :nk], v_blk)
             + jnp.einsum('bhnqs,bshd->bnqhd', p[..., nk:], v_ctx))
        return o.reshape(B, GRID_W, H, d)

    o = lax.map(one_row, jnp.arange(rows))
    return o.transpose(1, 0, 2, 3, 4).reshape(B, T, H * d)

def peer_ffn(h, wq, keys, u, v):
    B, T, D = h.shape
    x = h.reshape(B * T, D)
    n = x.shape[0]
    q = (x @ wq).reshape(n, PEER_HEADS, 2, PEER_DQ // 2)
    s = jnp.einsum('nhcd,hckd->nhck', q, keys).astype(jnp.float32)
    s1, i1 = lax.top_k(s[:, :, 0], PEER_TOPK)
    s2, i2 = lax.top_k(s[:, :, 1], PEER_TOPK)
    cand = (s1[..., :, None] + s2[..., None, :]).reshape(n, PEER_HEADS, PEER_TOPK * PEER_TOPK)
    sc, ci = lax.top_k(cand, PEER_TOPK)
    e = (jnp.take_along_axis(i1, ci // PEER_TOPK, axis=-1) * N_KEYS
         + jnp.take_along_axis(i2, ci % PEER_TOPK, axis=-1))
    g = jax.nn.softmax(sc, axis=-1)
    nb = n // PEER_TOK_BLOCK
    hk = PEER_HEADS * PEER_TOPK

    def one(args):
        xb, eb, gb = args
        a = jax.nn.gelu(jnp.einsum('tkd,td->tk', u[eb], xb))
        return jnp.einsum('tk,tkd->td', (a * gb.astype(a.dtype)), v[eb])

    y = lax.map(one, (x.reshape(nb, PEER_TOK_BLOCK, D), e.reshape(nb, PEER_TOK_BLOCK, hk),
                      g.reshape(nb, PEER_TOK_BLOCK, hk)))
    return y.reshape(B, T, D)

def trunk_layer(x, mod, l, ctx, w_in, w_out, norm_g, na_rpb, diff_lambda, diff_subln,
                gqa_qk_norm, peer_wq, peer_keys, peer_u, peer_v):
    B, T, _ = x.shape
    latent = ctx is not None
    shift1, scale1, gate1, shift2, scale2, gate2 = jnp.split(mod, 6, axis=-1)
    h = rms_norm(x, norm_g[l, 0]) * (1 + scale1) + shift1
    (aq, ak, av), (bq, bk, bv), (cq, ck, cv) = mixer_qkv(h, w_in[l], gqa_qk_norm[l], latent)
    lam_init = 0.8 - 0.6 * math.exp(-0.3 * l)
    lq = diff_lambda[l].astype(jnp.float32)
    lam = jnp.exp(jnp.sum(lq[0] * lq[1])) - jnp.exp(jnp.sum(lq[2] * lq[3])) + lam_init
    if latent:
        ka, va, kb, vb, kc, vc = ctx
        oa = neighbourhood_attend(aq, ak, av, ka, va, na_rpb[l])
        ob = diff_attend(bq, jnp.concatenate([bk, kb], axis=1), jnp.concatenate([bv, vb], axis=1), lam)
        oc = gqa_attend(cq, jnp.concatenate([ck, kc], axis=1), jnp.concatenate([cv, vc], axis=1))
    else:
        oa = gqa_attend(aq, ak, av)
        ob = diff_attend(bq, bk, bv, lam)
        oc = gqa_attend(cq, ck, cv)
    ob = (rms_norm(ob, diff_subln[l]) * (1 - lam_init)).reshape(B, T, H_B * DV_B)
    o = jnp.concatenate([oa, ob, oc], axis=-1) @ w_out[l]
    x = x + gate1 * o
    h2 = rms_norm(x, norm_g[l, 1]) * (1 + scale2) + shift2
    x = x + gate2 * peer_ffn(h2, peer_wq[l], peer_keys[l], peer_u[l], peer_v[l])
    return x, (ak, av, bk, bv, ck, cv)

def setup_inputs(seed: int = 0) -> dict:
    key = jax.random.key(seed)
    ks = jax.random.split(key, 24)
    f32 = jnp.float32

    def nrm(k, shape, s=1.0):
        return jax.random.normal(k, shape, f32) * s

    return {
        "x_prompt": nrm(ks[0], (BATCH, SEQ, D_MODEL)),
        "x_sample": nrm(ks[1], (DEC_BATCH, DEC_SEQ, D_MODEL)),
        "cache_a_k": nrm(ks[2], (DEC_BATCH, DEPTH, PAST_LEN, H_A, HEAD_DIM)),
        "cache_a_v": nrm(ks[3], (DEC_BATCH, DEPTH, PAST_LEN, H_A, HEAD_DIM)),
        "cache_b_k": nrm(ks[4], (DEC_BATCH, DEPTH, PAST_LEN, H_B, 2, DQK_B)),
        "cache_b_v": nrm(ks[5], (DEC_BATCH, DEPTH, PAST_LEN, H_B, DV_B)),
        "cache_c_k": nrm(ks[6], (DEC_BATCH, DEPTH, PAST_LEN, KV_C, HEAD_DIM)),
        "cache_c_v": nrm(ks[7], (DEC_BATCH, DEPTH, PAST_LEN, KV_C, HEAD_DIM)),
        "c": nrm(ks[8], (DEC_BATCH, D_MODEL)),
        "c_ctx": nrm(ks[9], (D_MODEL,)),
        "w_mod": nrm(ks[10], (DEPTH, D_MODEL, 6 * D_MODEL), 0.5 * D_MODEL ** -0.5),
        "b_mod": nrm(ks[11], (DEPTH, 6 * D_MODEL), 0.02),
        "norm_g": 1.0 + nrm(ks[12], (DEPTH, 2, D_MODEL), 0.1),
        "w_in": nrm(ks[13], (DEPTH, D_MODEL, IN_WIDTH), D_MODEL ** -0.5),
        "w_out": nrm(ks[14], (DEPTH, MIX_WIDTH, D_MODEL), MIX_WIDTH ** -0.5),
        "na_rpb": nrm(ks[15], (DEPTH, H_A, 2 * NA_ROWS - 1, 2 * NA_COLS - 1), 0.1),
        "diff_lambda": nrm(ks[16], (DEPTH, 4, DQK_B), 0.1),
        "diff_subln": 1.0 + nrm(ks[17], (DEPTH, DV_B), 0.1),
        "gqa_qk_norm": 1.0 + nrm(ks[18], (DEPTH, 2, HEAD_DIM), 0.1),
        "peer_wq": nrm(ks[19], (DEPTH, D_MODEL, PEER_HEADS * PEER_DQ), D_MODEL ** -0.5),
        "peer_keys": nrm(ks[20], (DEPTH, PEER_HEADS, 2, N_KEYS, PEER_DQ // 2), (PEER_DQ // 2) ** -0.5),
        "peer_u": nrm(ks[21], (DEPTH, N_EXPERTS, D_MODEL), D_MODEL ** -0.5),
        "peer_v": nrm(ks[22], (DEPTH, N_EXPERTS, D_MODEL), PEER_HEADS ** -0.5),
        "final_g": 1.0 + nrm(ks[23], (D_MODEL,), 0.1),
    }

def reference(x_prompt, x_sample, cache_a_k, cache_a_v, cache_b_k, cache_b_v, cache_c_k, cache_c_v,
              c, c_ctx, w_mod, b_mod, norm_g, w_in, w_out, na_rpb, diff_lambda, diff_subln,
              gqa_qk_norm, peer_wq, peer_keys, peer_u, peer_v, final_g):
    weights = (w_in, w_out, norm_g, na_rpb, diff_lambda, diff_subln, gqa_qk_norm,
               peer_wq, peer_keys, peer_u, peer_v)
    xp = x_prompt
    new_kv = []
    for l in range(DEPTH):
        mod_ctx = (jax.nn.silu(c_ctx) @ w_mod[l] + b_mod[l])[None, None, :]
        xp, kv = trunk_layer(xp, mod_ctx, l, None, *weights)
        new_kv.append(kv)
    y_prompt = rms_norm(xp, final_g)
    new_a_k = jnp.stack([kv[0] for kv in new_kv], axis=1)
    new_a_v = jnp.stack([kv[1] for kv in new_kv], axis=1)
    new_b_k = jnp.stack([kv[2] for kv in new_kv], axis=1)
    new_b_v = jnp.stack([kv[3] for kv in new_kv], axis=1)
    new_c_k = jnp.stack([kv[4] for kv in new_kv], axis=1)
    new_c_v = jnp.stack([kv[5] for kv in new_kv], axis=1)
    xs = x_sample
    for l in range(DEPTH):
        mod_lat = (jax.nn.silu(c) @ w_mod[l] + b_mod[l])[:, None, :]
        ctx = (cache_a_k[:, l], cache_a_v[:, l], cache_b_k[:, l], cache_b_v[:, l],
               cache_c_k[:, l], cache_c_v[:, l])
        xs, _ = trunk_layer(xs, mod_lat, l, ctx, *weights)
    y_sample = rms_norm(xs, final_g)
    return (y_prompt, y_sample, new_a_k, new_a_v, new_b_k, new_b_v, new_c_k, new_c_v)


_drawn_inputs = setup_inputs


def setup_inputs(seed=0):
    import zlib

    import numpy as np

    out = dict(_drawn_inputs(seed))
    spreads = {}
    factors = {'cache_a_k': 3.011,
     'cache_c_k': 6.179,
     'cache_c_v': 5.4,
     'na_rpb': 8.0,
     'diff_lambda': 6.379,
     'diff_subln': 2.975}
    for name, (base, spread) in spreads.items():
        noise = np.random.default_rng([zlib.crc32(name.encode()), seed]).standard_normal(out[name].shape)
        drawn = base * np.exp(spread * noise) if base else spread * noise
        out[name] = jnp.asarray(drawn.astype(out[name].dtype))
    for name, factor in factors.items():
        out[name] = (out[name] * factor).astype(out[name].dtype)
    return out
```

```python
import math
from contextlib import ExitStack

import numpy as np

import concourse.bass as bass
from concourse import mybir

F32 = mybir.dt.float32
U32 = mybir.dt.uint32
ALU = mybir.AluOpType
ACT = mybir.ActivationFunctionType
AX_X = mybir.AxisListType.X

P = 128
D = 1024
KC = D // P
L = 2
NLAT, NCTX = 512, 128
TOK = NLAT + NCTX
TT = TOK // P
GRID_W, ROWS = 64, NLAT // 64
EPS = 1e-6
NEG = -1.0e30
LOWEST = -3.0e38
CQ, CK, BQ, BK, AQ, AK = 0, 3, 4, 6, 8, 11
NQK = 14
VW = 768
NV = VW // P
NWIN = NQK + NV
B_SCALE = 32.0 ** -0.5
BROWS = 14
HEADS, TOPK, NK = 8, 16, 128
HC = 2 * HEADS
NGROUP, GJ = 16, 8
NU = NGROUP * GJ
EXP_AFTER = 6
NMOD = 48
RING = 8
POSTS = 12
GTOK, GB = 16, 4
GTURNS = P // GTOK

CONSTS = [("ident", 128), ("ones", 128), ("pairsum", 128), ("rotB", 128), ("rotC", 128),
          ("iota", 128), ("iota16", 16), ("mask", 64)]
TABLES = [("cosC", 512), ("sinC", 512), ("cosB", 512), ("sinB", 512)]
COLS = [("bmod", L * NMOD), ("gain", L * 2 * KC), ("fgain", KC), ("qkgain", L * 2), ("subln", L)]


def offsets(parts):
    out, at = {}, 0
    for name, n in parts:
        out[name] = at
        at += n
    return out, at


CO, NCONST = offsets(CONSTS)
TO, NTABLE = offsets(TABLES)
FO, NCOLS = offsets(COLS)


def attention_plan():
    maps, items, units = [], [], []
    for kind, chunks in (("A", 3), ("B", 2), ("C", 3)):
        for ch in range(chunks):
            for t in range(TT):
                for hh in range(2):
                    per = 2 if kind == "B" else 1
                    for c in range(per):
                        if kind == "A":
                            q, k, kp, kn, cc = AQ + ch, AK + ch, 64 * hh, 64, 3 + ch
                        elif kind == "B":
                            m = 2 * (2 * ch + hh) + c
                            q, k, kp, kn, cc = BQ + m // 4, BK + m // 4, 32 * (m % 4), 32, 1 + m // 4
                        else:
                            q, k, kp, kn, cc = CQ + ch, CK, 64 * hh, 64, 0
                        maps.append(dict(kind=kind, q=q, k=k, kp=kp, kn=kn, cc=cc, t=t, c=c,
                                         head=2 * ch + hh, item=len(items)))
                    vcol = {"A": 64 * (2 * ch + hh), "B": 384 + 64 * (2 * ch + hh), "C": 640 + 64 * hh}[kind]
                    items.append(dict(kind=kind, t=t, hh=hh, vcol=vcol, last=len(maps) - 1,
                                      first=len(maps) - per, unit=len(units)))
                units.append(dict(t=t, chunk={"A": 0, "B": 3, "C": 5}[kind] + ch, last=len(items) - 1))
    return maps, items, units


MAPS, ITEMS, UNITS = attention_plan()
NMAP, NITEM, NUNIT = len(MAPS), len(ITEMS), len(UNITS)
BY_LAST = {it["last"]: i for i, it in enumerate(ITEMS)}
UNIT_BY_LAST = {ITEMS[u["last"]]["last"]: i for i, u in enumerate(UNITS)}
SCALED = {m: i for i, m in enumerate([m for m, x in enumerate(MAPS) if x["kind"] != "B" or x["c"] == 1])}
MIXED = {i: n for n, i in enumerate([i for i, x in enumerate(ITEMS) if x["kind"] == "B"])}
NSCALED, NMIXED = len(SCALED), len(MIXED)

FIRST_MOD = 16
MOD_IN = [[(l, m) for m in range(FIRST_MOD, NMOD)] + [(l + 1, m) for m in range(FIRST_MOD) if l + 1 < L]
          for l in range(L)]


def block_plan():
    plan = [("mod", 0, m) for m in range(FIRST_MOD)]
    for l in range(L):
        plan += [("win", l, i) for i in range(NWIN)]
        plan += [("mod", a, m) for a, m in MOD_IN[l]]
        plan += [("wout", l, i) for i in range(KC)]
        plan += [("wq", l, i) for i in range(HC)]
        plan += [("ex", l, i) for i in range(NGROUP * 2 * GJ)]
    return {key: n for n, key in enumerate(plan)}


BLOCK = block_plan()


def build(nc, a):
    with ExitStack() as ctx:
        def sb(name, shape, dt=F32):
            return ctx.enter_context(nc.sbuf_tensor(name, shape, dt))

        def sem(name):
            return ctx.enter_context(nc.semaphore(name))

        xT = sb("xT", [P, KC, TOK])
        hT = sb("hT", [P, KC, TOK])
        oT = hT
        ring = sb("ring", [P, RING, KC, P])
        const = sb("const", [P, NCONST])
        cols = sb("cols", [P, NCOLS])
        modT = sb("modT", [P, L, NMOD, 2])
        cT = sb("cT", [P, KC, 2])
        cexp = sb("cexp", [P, KC, 2])
        lam = sb("lam", [P, L, 4, 32])
        lprod = sb("lprod", [P, L, 2, 32])
        lsum = sb("lsum", [P, L, 2])
        nlam = sb("nlam", [P, L])
        stat = sb("stat", [P, 12])
        WORK = 33100
        work = sb("work", [P, WORK])

        def at(off, *shape):
            n = int(np.prod(shape))
            assert off + n <= WORK
            ap = work[:, off:off + n]
            names = "abcd"[:len(shape)]
            if len(shape) > 1:
                ap = ap.rearrange(f"p ({' '.join(names)}) -> p {' '.join(names)}",
                                  **{x: s for x, s in zip(names, shape)})
            return ap

        qk = at(0, NQK, TOK)
        o = NQK * TOK
        vN = at(o, TT, VW); o += TT * VW
        kc = at(o, 6, P); o += 6 * P
        vc = at(o, VW); o += VW
        bias = at(o, 6, BROWS, GRID_W); o += 6 * BROWS * GRID_W
        table = at(o, NTABLE); o += NTABLE
        prob = at(o, 4, TOK); o += 4 * TOK
        probT = at(o, 2, TOK); o += 2 * TOK
        sq = at(o, 2, TOK); o += 2 * TOK
        var = at(o, TOK); o += TOK
        rs = at(o, TOK); o += TOK
        scores = at(0, TT, HC, P)
        o = TT * HC * P
        alt = at(o, HC * P); cand = at(o + HC * P, HC * P); o += 2 * HC * P
        gst = at(o, P, P)
        keys = at(o, HC, P)
        qTb = at(o + HC * P, 2, TOK)
        o += P * P
        top = at(o, HEADS, 2, TOPK); o += 256
        topi = at(o, HEADS * 2 * TOPK).bitcast(U32); o += 256
        topf = at(o, HEADS, 2, TOPK); o += 256
        sel = at(o, P); o += P
        seli = at(o, P).bitcast(U32); o += P
        hi = at(o, P).bitcast(U32); o += P
        route = at(o, 3, P); o += 3 * P
        routeT = at(o, 3, P); o += 3 * P
        gsum = at(o, 2 * HEADS); o += 2 * HEADS
        oneh1 = alt.rearrange("p (t i) -> p t i", i=P)
        oneh2 = cand.rearrange("p (t i) -> p t i", i=P)
        hid = [at(i * GJ * TOK, GJ, TOK) for i in range(2)]
        gate = [at((2 + i) * GJ * TOK, GJ, TOK) for i in range(2)]

        psum = ctx.enter_context(nc.psum_tensor("psum", [P, 8, 512], F32))
        pair = [psum[:, 2 * i:2 * i + 2, :].rearrange("p b n -> p (b n)") for i in range(4)]
        modps = psum[:, 7, 0:L * NMOD * 2].rearrange("p (l m s) -> p l m s", l=L, s=2)

        def con(name, p=P):
            return const[0:p, CO[name]:CO[name] + dict(CONSTS)[name]]

        def tab(name):
            return table[:, TO[name]:TO[name] + 512]

        def col(name, i):
            return cols[:, FO[name] + i:FO[name] + i + 1]

        gdram = nc.dram_tensor("gate_matrix", (P, P, TOK), F32, kind="Internal").ap()

        hdram = nc.dram_tensor("hidden", (P, P, TOK), F32, kind="Internal").ap()
        xdram = nc.dram_tensor("residual", (P, KC, TOK), F32, kind="Internal").ap()

        inputs_in = sem("inputs_in")
        landed = [sem(f"landed{i}") for i in range(RING)]
        block_done = sem("block_done")
        c_sq = sem("c_sq")
        b_sq = sem("b_sq")
        dve_chain = sem("dve_chain")
        silu_exp = sem("silu_exp")
        c_ready = sem("c_ready")
        lam_sum = sem("lam_sum")
        lam_exp = sem("lam_exp")
        lam_ready = sem("lam_ready")
        mod_ready = sem("mod_ready")
        sq_ready = sem("sq_ready")
        sum_step = sem("sum_step")
        var_ready = sem("var_ready")
        sd_ready = sem("sd_ready")
        h_ready = sem("h_ready")
        proj_evac = sem("proj_evac")
        post_mm = sem("post_mm")
        post_fin = sem("post_fin")
        layer_in = sem("layer_in")
        bias_in = sem("bias_in")
        bias_ready = sem("bias_ready")
        kv_stored = sem("kv_stored")
        score_done = sem("score_done")
        max_done = sem("max_done")
        exp_done = sem("exp_done")
        rinv_done = sem("rinv_done")
        scaled = sem("scaled")
        mixed = sem("mixed")
        tr_done = sem("tr_done")
        pt_done = sem("pt_done")
        pv_done = sem("pv_done")
        o_evac = sem("o_evac")
        bn_mm = sem("bn_mm")
        bn_fin = sem("bn_fin")
        wout_added = sem("wout_added")
        keys_in = sem("keys_in")
        keyscore = sem("keyscore")
        scores_in = sem("scores_in")
        sub_ready = sem("sub_ready")
        gexp_ready = sem("gexp_ready")
        route_ready = sem("route_ready")
        route_tr = sem("route_tr")
        route_in = sem("route_in")
        onehot = sem("onehot")
        g_mm = [sem(f"g_mm{q}") for q in range(GB)]
        g_evac = [sem(f"g_evac{q}") for q in range(GB)]
        g_stored = sem("g_stored")
        hid_out = [sem(f"hid_out{i}") for i in range(GJ)]
        x_out = sem("x_out")
        x_in = sem("x_in")
        g_landed = [sem(f"g_landed{i}") for i in range(2)]
        gelu_done = sem("gelu_done")
        hid_ready = sem("hid_ready")
        y_added = sem("y_added")
        y_ready = sem("y_ready")
        y_stored = sem("y_stored")

        PROJ = NWIN + HC
        NORMS = 2 * L + 1
        ROOTS = 2 + 4 + 2

        def roots(l, i):
            return l * ROOTS + i + 1

        N_INPUTS = 5
        block = ctx.enter_context(nc.Block())

        @block.sync
        def _(sp):
            for dst, src in ((cT[:], a["cT"]), (const[:], a["const"]), (cols[:], a["cols"]), (xT[:], a["xT"]),
                             (lam[:], a["lam"].partition_broadcast(P))):
                sp.dma_start(dst, src).then_inc(inputs_in, 16)

            def load(n, src):
                if n >= RING:
                    sp.wait_ge(block_done, n - RING + 1)
                sp.dma_start(ring[:, n % RING], src).then_inc(landed[n % RING], 16)

            def hidden_pass(l):
                n0 = BLOCK["ex", l, 0]
                src = a["expert"][l]

                def store(i, k):
                    sp.wait_ge(gelu_done, i * GJ + (NU * l + k + 1))
                    sp.dma_start(hdram[bass.ds(i * GJ + k, 1)].rearrange("o i t -> i (o t)"), xT[:, k, :]).then_inc(hid_out[k], 16)

                def turn(i):
                    for k in range(GJ):
                        n = n0 + k
                        sp.wait_ge(block_done, i * GJ + (n - RING + 1))
                        sp.dma_start(ring[:, n % RING], src[i * GJ + k]).then_inc(landed[n % RING], 16)
                        if not isinstance(i, int) or i * GJ + k >= GJ + 1:
                            store(*((i - 1, k - 1) if k else (i - 2, GJ - 1)))

                for k in range(GJ):
                    load(n0 + k, src[k])
                sp.wait_ge(h_ready, 2 * l + 2)
                sp.dma_start(xdram, xT[:]).then_inc(x_out, 16)
                turn(1)
                with sp.Fori(2, NGROUP) as i:
                    turn(i)
                return store

            def output_pass(l, store):
                n0 = BLOCK["ex", l, NU]
                src = a["expert"][l]

                def inputs(g, b):
                    for k in range(GJ):
                        sp.wait_ge(hid_out[k], g * 16 + 16 * (NGROUP * l + 1))
                    sp.dma_start(hid[b], group(hdram, g)).then_inc(g_landed[b], 16)
                    sp.dma_start(gate[b], group(gdram, g)).then_inc(g_landed[b], 16)

                def group(t, g):
                    return t.rearrange("(g j) i t -> g i j t", j=GJ)[g]

                store(NGROUP - 2, GJ - 1)
                sp.wait_ge(g_stored, 16 * TT * (l + 1))
                inputs(0, 0)
                inputs(1, 1)
                for k in range(GJ):
                    load(n0 + k, src[NU + k])
                    store(NGROUP - 1, k)
                for k in range(GJ):
                    sp.wait_ge(hid_out[k], 16 * NGROUP * (l + 1))
                sp.dma_start(xT[:], xdram).then_inc(x_in, 16)

                def step(g, b):
                    for k in range(GJ):
                        n = n0 + k
                        sp.wait_ge(block_done, g * GJ + (n - RING + 1))
                        sp.dma_start(ring[:, n % RING], src[NU + g * GJ + k]).then_inc(landed[n % RING], 16)
                    sp.wait_ge(block_done, g * GJ + n0)
                    inputs(g + 1, 1 - b)

                with sp.Fori(0, (NGROUP - 2) // 2) as i:
                    step(i * 2 + 1, 1)
                    step(i * 2 + 2, 0)
                for k in range(GJ):
                    load(n0 + (NGROUP - 1) * GJ + k, src[NU + (NGROUP - 1) * GJ + k])

            for m in range(FIRST_MOD):
                load(BLOCK["mod", 0, m], a["w_mod"][0, m])
            for l in range(L):
                for i in range(NWIN):
                    load(BLOCK["win", l, i], a["w_in"][l, i])
                for b, m in MOD_IN[l]:
                    load(BLOCK["mod", b, m], a["w_mod"][b, m])
                for i in range(KC):
                    load(BLOCK["wout", l, i], a["w_out"][l, i])
                for i in range(HC):
                    load(BLOCK["wq", l, i], a["w_query"][l, i])
                output_pass(l, hidden_pass(l))
            sp.wait_ge(y_ready, 1)
            sp.dma_start(a["out_yT"], hT[:]).then_inc(y_stored, 16)
            sp.wait_ge(y_stored, 16)
            sp.wait_ge(kv_stored, 16 * 4 * L)

        @block.tensor
        def _(pe):
            def take(n):
                pe.wait_ge(landed[n % RING], 16 * (n // RING + 1))
                return ring[:, n % RING]

            def wide(out, lhsT_of, rhs_of, ks, width=TOK):
                for lo, hi_ in ((0, 512), (512, width)):
                    if lo >= hi_:
                        continue
                    for k in range(ks):
                        last = pe.matmul(out[:, lo:hi_], lhsT_of(k), rhs_of(k)[:, lo:hi_],
                                         start=(k == 0), stop=(k == ks - 1))
                return last

            def mod_block(l, m):
                n = BLOCK["mod", l, m]
                w = take(n)
                for k in range(KC):
                    last = pe.matmul(modps[:, l, m, :], w[:, k, :], cT[:, k, :], start=(k == 0), stop=(k == KC - 1))
                last.then_inc(block_done, 1)

            def norm(ni):
                for c in range(KC):
                    pe.wait_ge(sq_ready, KC * ni + c + 1)
                    for lo, hi_ in ((0, 512), (512, TOK)):
                        last = pe.matmul(pair[0][:, lo:hi_], con("ones"), sq[:, c % 2, lo:hi_],
                                         start=(c == 0), stop=(c == KC - 1))
                    last.then_inc(sum_step, 1)

            def post(l, p):
                if POSTS * l + p > 0:
                    pe.wait_ge(post_fin, POSTS * l + p)
                if p < 4:
                    pe.wait_ge(c_sq, 4 * l + p + 1)
                    wide(pair[2], lambda k: con("pairsum"), lambda k: sq[:, p % 2, :], 1).then_inc(post_mm, 1)
                else:
                    ch = p - 4
                    pe.wait_ge(proj_evac, PROJ * l + ch + 1)
                    rot = con("rotC" if ch < BQ else "rotB")
                    pe.matmul(pair[2][:, 0:NLAT], rot, qk[:, ch, 0:NLAT], start=True, stop=True).then_inc(post_mm, 1)

            def project(l):
                pe.wait_ge(h_ready, 2 * l + 1)
                for i in range(NWIN):
                    if i >= 2:
                        pe.wait_ge(proj_evac, PROJ * l + i - 1)
                    w = take(BLOCK["win", l, i])
                    out = pair[i % 2]
                    if i < NQK:
                        last = wide(out, lambda k: w[:, k, :], lambda k: hT[:, k, :], KC)
                    else:
                        for t in range(TT):
                            for k in range(KC):
                                last = pe.matmul(out[:, t * P:(t + 1) * P], hT[:, k, t * P:(t + 1) * P], w[:, k, :],
                                                 start=(k == 0), stop=(k == KC - 1))
                    last.then_inc(block_done, 1)
                    if 4 <= i < 4 + POSTS:
                        post(l, i - 4)

            def attention(l):
                pe.wait_ge(proj_evac, PROJ * l + NWIN)
                pe.wait_ge(post_fin, POSTS * (l + 1))
                pe.wait_ge(layer_in, 16 * 3 * (l + 1))
                extra = list(MOD_IN[l])
                for n in range(NMAP + 3):
                    if n < NMAP:
                        m = MAPS[n]
                        ps = pair[n % 2]
                        if n >= 2:
                            pe.wait_ge(exp_done, NMAP * l + n - 1)
                        kp, kn, t = m["kp"], m["kn"], m["t"]
                        q = qk[kp:kp + kn, m["q"], t * P:(t + 1) * P]
                        if t < TT - 1:
                            pe.matmul(ps[:, 0:NLAT], q, qk[kp:kp + kn, m["k"], 0:NLAT], start=True, stop=True)
                            last = pe.matmul(ps[:, NLAT:TOK], q, kc[kp:kp + kn, m["cc"], :], start=True, stop=True)
                        else:
                            last = pe.matmul(ps[:, 0:NCTX], q, qk[kp:kp + kn, m["k"], NLAT:TOK], start=True, stop=True)
                        last.then_inc(score_done, 1)
                        if n % 2 == 0 and extra:
                            mod_block(*extra.pop(0))
                    if n - 2 in BY_LAST:
                        i = BY_LAST[n - 2]
                        it = ITEMS[i]
                        if it["kind"] == "B":
                            pe.wait_ge(mixed, NMIXED * l + MIXED[i] + 1)
                        else:
                            pe.wait_ge(scaled, NSCALED * l + SCALED[n - 2] + 1)
                        if i > 0:
                            pe.wait_ge(pt_done, NITEM * l + i)
                        src = prob[:, it["first"] % 4, :]
                        for b in range(TT if it["t"] < TT - 1 else 1):
                            last = pe.transpose(pair[2][:, b * P:(b + 1) * P], src[:, b * P:(b + 1) * P], con("ident"))
                        last.then_inc(tr_done, 1)
                    if n - 3 in BY_LAST:
                        i = BY_LAST[n - 3]
                        it = ITEMS[i]
                        pe.wait_ge(pt_done, NITEM * l + i + 1)
                        if it["hh"] == 0 and it["unit"] > 0:
                            pe.wait_ge(o_evac, NUNIT * l + it["unit"])
                        out = psum[64 * it["hh"]:64 * it["hh"] + 64, 6, 0:P]
                        vs = slice(it["vcol"], it["vcol"] + 64)
                        pt = probT[:, i % 2, :]
                        if it["t"] < TT - 1:
                            for b in range(TT):
                                last = pe.matmul(out, vN[:, b, vs] if b < TT - 1 else vc[:, vs],
                                                 pt[:, b * P:(b + 1) * P], start=(b == 0), stop=(b == TT - 1))
                        else:
                            last = pe.matmul(out, vN[:, TT - 1, vs], pt[:, 0:P], start=True, stop=True)
                        last.then_inc(pv_done, 1)
                for b in range(2):
                    pe.wait_ge(b_sq, 2 * l + b + 1)
                    wide(pair[b], lambda k: con("pairsum"), lambda k: sq[:, b, :], 1).then_inc(bn_mm, 1)

            def out_projection(l):
                pe.wait_ge(bn_fin, 2 * (l + 1))
                pe.wait_ge(o_evac, NUNIT * (l + 1))
                for c in range(KC):
                    if c >= 2:
                        pe.wait_ge(wout_added, KC * l + c - 1)
                    w = take(BLOCK["wout", l, c])
                    wide(pair[c % 2], lambda k: w[:, k, :], lambda k: oT[:, k, :], KC).then_inc(block_done, 1)

            def queries(l):
                pe.wait_ge(h_ready, 2 * l + 2)
                pe.wait_ge(keys_in, 16 * (l + 1))
                for s in range(HC + 1):
                    if s < HC:
                        if s >= 2:
                            pe.wait_ge(proj_evac, PROJ * l + NWIN + s - 1)
                        w = take(BLOCK["wq", l, s])
                        wide(pair[s % 2], lambda k: w[:, k, :], lambda k: hT[:, k, :], KC).then_inc(block_done, 1)
                    if s >= 1:
                        r = s - 1
                        pe.wait_ge(proj_evac, PROJ * l + NWIN + r + 1)
                        if r >= 2:
                            pe.wait_ge(scores_in, HC * l + r - 1)
                        for t in range(TT):
                            last = pe.matmul(pair[2 + r % 2][:, t * P:(t + 1) * P], qTb[:, r % 2, t * P:(t + 1) * P],
                                             keys[:, r, :], start=True, stop=True)
                        last.then_inc(keyscore, 1)

            def hidden_pass(l):
                n0 = BLOCK["ex", l, 0]
                base = NU * l

                def u_block(i, k):
                    n = n0 + k
                    pe.wait_ge(landed[n % RING], i * 16 + 16 * (n // RING + 1))
                    w = ring[:, n % RING]
                    if not isinstance(i, int) or i * GJ + k >= 2:
                        pe.wait_ge(gelu_done, i * GJ + (base + k - 1))
                    wide(pair[k % 2], lambda c: w[:, c, :], lambda c: hT[:, c, :], KC).then_inc(block_done, 1)

                for t in range(TT):
                    tile = TT * l + t
                    for k in range(GJ):
                        u_block(3 * t, k)
                    pe.wait_ge(route_ready, tile + 1)
                    if t == 0:
                        pe.wait_ge(scores_in, HC * (l + 1))
                    else:
                        pe.wait_ge(g_evac[0], GTURNS * tile + 1)
                    for r in range(3):
                        last = pe.transpose(psum[:, 4, r * P:(r + 1) * P], route[:, r, :], con("ident"))
                    last.then_inc(route_tr, 1)
                    pe.wait_ge(route_in, tile + 1)
                    with pe.Fori(0, 2) as i:
                        for s4 in range(GTURNS // 2):
                            for q in range(GB):
                                if q % 2 == 0:
                                    u_block(i + (3 * t + 1), 2 * s4 + q // 2)
                                turn = i * (GTURNS // 2) + (GTURNS * tile + s4)
                                pe.wait_ge(onehot, turn * GB + (q + 1))
                                pe.wait_ge(g_evac[q], turn + 1)
                                for k in range(4):
                                    s = 4 * q + k
                                    last = pe.matmul(psum[:, 4 + q, k * P:(k + 1) * P], oneh1[:, s, :],
                                                     oneh2[:, s, :], start=True, stop=True)
                                last.then_inc(g_mm[q], 1)
                for k in range(GJ):
                    u_block(NGROUP - 1, k)

            def output_pass(l):
                n0 = BLOCK["ex", l, NU]
                base = NGROUP * KC * l

                def v_group(g, b):
                    pe.wait_ge(hid_ready, g * GJ + (base + GJ))
                    for c in range(KC):
                        n = n0 + c
                        pe.wait_ge(landed[n % RING], g * 16 + 16 * (n // RING + 1))
                        w = ring[:, n % RING]
                        if not isinstance(g, int) or g * KC + c >= 2:
                            pe.wait_ge(y_added, g * KC + (base + c - 1))
                        wide(pair[2 + c % 2], lambda j: w[:, j, :], lambda j: hid[b][:, j, :], GJ).then_inc(
                            block_done, 1)

                for q in range(GB):
                    pe.wait_ge(g_evac[q], GTURNS * TT * (l + 1) + 1)
                v_group(0, 0)
                with pe.Fori(0, (NGROUP - 2) // 2) as i:
                    v_group(i * 2 + 1, 1)
                    v_group(i * 2 + 2, 0)
                v_group(NGROUP - 1, 1)

            for q in range(GB):
                pe.sem_inc(g_mm[q], 1)
            pe.wait_ge(inputs_in, 16 * N_INPUTS)
            pe.wait_ge(c_ready, 1)
            for m in range(FIRST_MOD):
                mod_block(0, m)
            for l in range(L):
                norm(2 * l)
                project(l)
                attention(l)
                out_projection(l)
                norm(2 * l + 1)
                queries(l)
                hidden_pass(l)
                output_pass(l)
            norm(2 * L)

        @block.scalar
        def _(act):
            act.wait_ge(inputs_in, 16 * N_INPUTS)
            act.activation(cexp[:], cT[:], ACT.Exp, scale=-1.0).then_inc(silu_exp, 1)
            act.wait_ge(lam_sum, 1)
            act.activation(lsum[:], lsum[:], ACT.Exp).then_inc(lam_exp, 1)

            def norm(ni):
                if ni % 2 == 1:
                    act.wait_ge(wout_added, KC * (ni // 2 + 1))
                elif ni > 0:
                    act.wait_ge(y_added, NGROUP * KC * (ni // 2))
                for c in range(KC):
                    if c >= 2:
                        act.wait_ge(sum_step, KC * ni + c - 1)
                    act.activation(sq[:, c % 2, :], xT[:, c, :], ACT.Square).then_inc(sq_ready, 1)
                root(*((ni // 2, 0) if ni % 2 == 0 else (ni // 2, 7)))

            def root(l, i):
                act.wait_ge(var_ready, roots(l, i))
                act.activation(var, var, ACT.Sqrt).then_inc(sd_ready, 1)

            def project(l):
                for i in range(NWIN):
                    act.wait_ge(block_done, BLOCK["win", l, i] + 1)
                    src = pair[i % 2][:, 0:TOK]
                    if i < NQK:
                        scale = B_SCALE if BQ <= i < BK else 0.125 if AQ <= i < AK else 1.0
                        act.activation(qk[:, i, :], src, ACT.Copy, scale=scale).then_inc(proj_evac, 1)
                    else:
                        m = i - NQK
                        act.activation(vN[:, :, m * P:(m + 1) * P], src.rearrange("p (t d) -> p t d", t=TT),
                                       ACT.Copy).then_inc(proj_evac, 1)
                    if 3 <= i < 7:
                        r = i - 3
                        act.wait_ge(proj_evac, PROJ * l + r + 1)
                        if r >= 2:
                            act.wait_ge(post_mm, POSTS * l + r - 1)
                        act.activation(sq[:, r % 2, :], qk[:, r, :], ACT.Square).then_inc(c_sq, 1)
                    if 5 <= i < 9:
                        root(l, 1 + i - 5)

            def attention(l):
                for n in range(NMAP + 3):
                    if n < NMAP:
                        m = MAPS[n]
                        w = TOK if m["t"] < TT - 1 else NCTX
                        act.wait_ge(max_done, NMAP * l + n + 1)
                        if n >= 4:
                            act.wait_ge(tr_done, NITEM * l + MAPS[n - 4]["item"] + 1)
                        act.activation(prob[:, n % 4, 0:w], pair[n % 2][:, 0:w], ACT.Exp,
                                       bias=stat[:, n % 4:n % 4 + 1],
                                       accum_out=stat[:, 4 + n % 4:5 + n % 4]).then_inc(exp_done, 1)
                    if n - 2 in BY_LAST:
                        i = BY_LAST[n - 2]
                        w = TOK if ITEMS[i]["t"] < TT - 1 else NCTX
                        act.wait_ge(tr_done, NITEM * l + i + 1)
                        if i >= 2:
                            act.wait_ge(pv_done, NITEM * l + i - 1)
                        act.activation(probT[:, i % 2, 0:w], pair[2][:, 0:w], ACT.Copy).then_inc(pt_done, 1)
                    if n - 3 in UNIT_BY_LAST:
                        u = UNIT_BY_LAST[n - 3]
                        act.wait_ge(pv_done, NITEM * l + UNITS[u]["last"] + 1)
                        act.activation(oT[:, UNITS[u]["chunk"], UNITS[u]["t"] * P:(UNITS[u]["t"] + 1) * P],
                                       psum[:, 6, 0:P], ACT.Copy).then_inc(o_evac, 1)
                act.wait_ge(o_evac, NUNIT * (l + 1))
                for b in range(2):
                    act.activation(sq[:, b, :], oT[:, 3 + b, :], ACT.Square).then_inc(b_sq, 1)
                for b in range(2):
                    root(l, 5 + b)

            def queries(l):
                act.wait_ge(kv_stored, 16 * 4 * (l + 1))
                for s in range(HC + 1):
                    if s < HC:
                        act.wait_ge(block_done, BLOCK["wq", l, s] + 1)
                        if s >= 2:
                            act.wait_ge(keyscore, HC * l + s - 1)
                        act.activation(qTb[:, s % 2, :], pair[s % 2][:, 0:TOK], ACT.Copy).then_inc(proj_evac, 1)
                    if s >= 1:
                        r = s - 1
                        act.wait_ge(keyscore, HC * l + r + 1)
                        act.activation(scores[:, :, r, :],
                                       pair[2 + r % 2][:, 0:TOK].rearrange("p (t d) -> p t d", t=TT),
                                       ACT.Copy).then_inc(scores_in, 1)

            def hidden_pass(l):
                n0 = BLOCK["ex", l, 0]

                def gelu(i, k):
                    act.wait_ge(block_done, i * GJ + (n0 + k + 1))
                    if not isinstance(i, int) or NGROUP * l + i > 0:
                        act.wait_ge(hid_out[k], i * 16 + 16 * NGROUP * l)
                    act.activation(xT[:, k, :], pair[k % 2][:, 0:TOK], ACT.Gelu_apprx_tanh).then_inc(gelu_done, 1)

                act.wait_ge(x_out, 16 * (l + 1))
                for t in range(TT):
                    tile = TT * l + t
                    for k in range(GJ):
                        if k == EXP_AFTER:
                            act.wait_ge(sub_ready, tile + 1)
                            act.activation(sel, sel, ACT.Exp).then_inc(gexp_ready, 1)
                        gelu(3 * t, k)
                    act.wait_ge(route_tr, tile + 1)
                    act.activation(routeT, psum[:, 4, 0:3 * P].rearrange("p (r t) -> p r t", r=3),
                                   ACT.Copy).then_inc(route_in, 1)
                    if tile > 0:
                        act.wait_ge(g_stored, 16 * tile)
                    with act.Fori(0, 2) as i:
                        for s4 in range(GTURNS // 2):
                            for q in range(GB):
                                if q % 2 == 0:
                                    gelu(i + (3 * t + 1), 2 * s4 + q // 2)
                                turn = i * (GTURNS // 2) + (GTURNS * tile + s4)
                                act.wait_ge(g_mm[q], turn + 2)
                                dst = gst[:, :, bass.ds(i * (P // 2) + (s4 * GTOK + 4 * q), 4)]
                                act.activation(dst, psum[:, 4 + q, :].rearrange("p (t j) -> p j t", t=4),
                                               ACT.Copy).then_inc(g_evac[q], 1)
                    for q in range(GB):
                        act.wait_ge(g_evac[q], GTURNS * (tile + 1) + 1)
                    act.dma_start(gdram.rearrange("j i t -> i j t")[:, :, t * P:(t + 1) * P], gst).then_inc(g_stored, 16)
                for k in range(GJ):
                    gelu(NGROUP - 1, k)

            for q in range(GB):
                act.sem_inc(g_evac[q], 1)
            for l in range(L):
                norm(2 * l)
                project(l)
                attention(l)
                norm(2 * l + 1)
                queries(l)
                hidden_pass(l)
            norm(2 * L)

        @block.vector
        def _(dve):
            links = [0]

            def link(ins):
                links[0] += 1
                ins.then_inc(dve_chain, 1)
                dve.wait_ge(dve_chain, links[0])

            dve.wait_ge(silu_exp, 1)
            link(dve.tensor_scalar(cexp[:], cexp[:], 1.0, None, ALU.add))
            link(dve.reciprocal(cexp[:], cexp[:]))
            dve.tensor_tensor(cT[:], cT[:], cexp[:], ALU.mult).then_inc(c_ready, 1)
            link(dve.tensor_tensor(lprod[:], lam[:, :, 0:4:2, :], lam[:, :, 1:4:2, :], ALU.mult))
            dve.tensor_reduce(lsum[:], lprod[:], AX_X, ALU.add).then_inc(lam_sum, 1)
            dve.wait_ge(lam_exp, 1)
            link(dve.tensor_tensor(nlam[:], lsum[:, :, 1], lsum[:, :, 0], ALU.subtract))
            for l in range(L):
                init = 0.8 - 0.6 * math.exp(-0.3 * l)
                dve.tensor_scalar(nlam[:, l:l + 1], nlam[:, l:l + 1], -init, None, ALU.add).then_inc(lam_ready, 1)
                dve.tensor_scalar(col("qkgain", 2 * l), col("qkgain", 2 * l), 0.125, None, ALU.mult)
                link(dve.tensor_scalar(col("subln", l), col("subln", l), 1.0 - init, None, ALU.mult))

            def modulation(l, lo, hi_, after):
                dve.wait_ge(block_done, after + 1)
                b = cols[:, FO["bmod"] + NMOD * l + lo:FO["bmod"] + NMOD * l + hi_]
                link(dve.tensor_tensor(modT[:, l, lo:hi_, :], modps[:, l, lo:hi_, :],
                                       b.unsqueeze(2).to_broadcast([P, hi_ - lo, 2]), ALU.add))
                for half in range(2):
                    s = KC * (3 * half + 1)
                    if lo <= s < hi_:
                        gcol = FO["gain"] + KC * (2 * l + half)
                        link(dve.scalar_tensor_tensor(modT[:, l, s:s + KC, :], modT[:, l, s:s + KC, :], 1.0,
                                                      cols[:, gcol:gcol + KC].unsqueeze(2).to_broadcast([P, KC, 2]),
                                                      ALU.add, ALU.mult))

            def root(l, i, ps, n):
                dve.tensor_scalar(var, ps[:, 0:TOK], 1.0 / n, EPS, ALU.mult, ALU.add).then_inc(var_ready, 1)
                dve.wait_ge(sd_ready, roots(l, i))
                link(dve.reciprocal(rs, var))

            def norm(ni):
                l, half = ni // 2, ni % 2
                dve.wait_ge(sum_step, KC * (ni + 1))
                root(l, 7 if half else 0, pair[0], D)
                for c in range(KC):
                    last = dve.tensor_tensor(hT[:, c, :], xT[:, c, :], rs, ALU.mult)
                link(last)
                for c in range(KC):
                    if ni == 2 * L:
                        last = dve.tensor_scalar(hT[:, c, :], hT[:, c, :], col("fgain", c), None, ALU.mult)
                        continue
                    for s, (lo, hi_) in enumerate(((0, NLAT), (NLAT, TOK))):
                        m = 3 * KC * half + c
                        last = dve.tensor_scalar(hT[:, c, lo:hi_], hT[:, c, lo:hi_],
                                                 modT[:, l, m + KC, s:s + 1], modT[:, l, m, s:s + 1],
                                                 ALU.mult, ALU.add)
                last.then_inc(y_ready if ni == 2 * L else h_ready, 1)

            def posts(l):
                for p in range(POSTS):
                    dve.wait_ge(post_mm, POSTS * l + p + 1)
                    if p < 4:
                        root(l, 1 + p, pair[2], 64)
                        dve.scalar_tensor_tensor(qk[:, p, :], qk[:, p, :], col("qkgain", 2 * l + (p == 3)), rs,
                                                 ALU.mult, ALU.mult).then_inc(post_fin, 1)
                    else:
                        ch = p - 4
                        kind = "C" if ch < BQ else "B"
                        if p == 4:
                            dve.wait_ge(layer_in, 16 * 3 * (l + 1))
                        x = qk[:, ch, 0:NLAT]
                        dve.tensor_tensor(var[:, 0:NLAT], pair[2][:, 0:NLAT], tab("sin" + kind), ALU.mult)
                        link(dve.tensor_tensor(x, x, tab("cos" + kind), ALU.mult))
                        dve.tensor_tensor(x, x, var[:, 0:NLAT], ALU.add).then_inc(post_fin, 1)

            def attention(l):
                dve.wait_ge(bias_ready, 6 * (l + 1))
                for n in range(NMAP + 2):
                    if n < NMAP:
                        m = MAPS[n]
                        ps = pair[n % 2]
                        lat = m["t"] < TT - 1
                        dve.wait_ge(score_done, NMAP * l + n + 1)
                        if m["kind"] == "A" and lat:
                            r0 = 6 - 2 * m["t"]
                            b = bias[:, m["head"], r0:r0 + ROWS, :].rearrange("p r c -> p (r c)")
                            link(dve.tensor_tensor(ps[:, 0:NLAT], ps[:, 0:NLAT], b, ALU.add))
                        dve.tensor_reduce(stat[:, n % 4:n % 4 + 1], ps[:, 0:TOK if lat else NCTX], AX_X, ALU.max,
                                          negate=True).then_inc(max_done, 1)
                    if 1 <= n <= NMAP:
                        s = (n - 1) % 4
                        dve.wait_ge(exp_done, NMAP * l + n)
                        dve.reciprocal(stat[:, 8 + s:9 + s], stat[:, 4 + s:5 + s]).then_inc(rinv_done, 1)
                    if n - 2 in BY_LAST and ITEMS[BY_LAST[n - 2]]["kind"] == "B":
                        it = ITEMS[BY_LAST[n - 2]]
                        w = TOK if it["t"] < TT - 1 else NCTX
                        s0, s1 = it["first"] % 4, it["last"] % 4
                        dve.wait_ge(scaled, NSCALED * l + SCALED[n - 2] + 1)
                        dve.scalar_tensor_tensor(prob[:, s0, 0:w], prob[:, s0, 0:w], stat[:, 8 + s0:9 + s0],
                                                 prob[:, s1, 0:w], ALU.mult, ALU.add).then_inc(mixed, 1)
                after = BLOCK["mod", *MOD_IN[l][-1]]
                modulation(l, FIRST_MOD, NMOD, after)
                if l + 1 < L:
                    modulation(l + 1, 0, FIRST_MOD, after)
                for b in range(2):
                    dve.wait_ge(bn_mm, 2 * l + b + 1)
                    root(l, 5 + b, pair[b], 64)
                    dve.scalar_tensor_tensor(oT[:, 3 + b, :], oT[:, 3 + b, :], col("subln", l), rs,
                                             ALU.mult, ALU.mult).then_inc(bn_fin, 1)

            def residual(ps, c, l, m):
                for s, (lo, hi_) in enumerate(((0, NLAT), (NLAT, TOK))):
                    last = dve.scalar_tensor_tensor(xT[:, c, lo:hi_], ps[:, lo:hi_], modT[:, l, m + c, s:s + 1],
                                                    xT[:, c, lo:hi_], ALU.mult, ALU.add)
                return last

            def out_projection(l):
                for c in range(KC):
                    dve.wait_ge(block_done, BLOCK["wout", l, c] + 1)
                    residual(pair[c % 2], c, l, 2 * KC).then_inc(wout_added, 1)

            def top16(src, spare, vals, idx, n, width):
                for r in range(n):
                    last = dve.max(vals[r][:, 0:8], src[r])
                link(last)
                for r in range(n):
                    dve.max_index(idx[r][:, 0:8], vals[r][:, 0:8], src[r])
                    last = dve.match_replace(spare[r], vals[r][:, 0:8], src[r], LOWEST)
                link(last)
                for r in range(n):
                    last = dve.max(vals[r][:, 8:16], spare[r])
                link(last)
                for r in range(n):
                    last = dve.max_index(idx[r][:, 8:16], vals[r][:, 8:16], spare[r])
                link(last)

            def gates(l):
                for t in range(TT):
                    tile = TT * l + t
                    if t == 0:
                        dve.wait_ge(scores_in, HC * (l + 1))
                    else:
                        for q in range(GB):
                            dve.wait_ge(g_mm[q], GTURNS * tile + 1)
                    topr = top.rearrange("p h c k -> p (h c) k")
                    topir = topi.rearrange("p (r k) -> p r k", k=TOPK)
                    altr = alt.rearrange("p (r k) -> p r k", k=P)
                    top16([scores[:, t, r, :] for r in range(HC)], [altr[:, r, :] for r in range(HC)],
                          [topr[:, r, :] for r in range(HC)], [topir[:, r, :] for r in range(HC)], HC, P)
                    c4 = cand.rearrange("p (h a b) -> p h a b", h=HEADS, a=TOPK)
                    link(dve.tensor_tensor(c4, top[:, :, 0, :].unsqueeze(3).to_broadcast([P, HEADS, TOPK, TOPK]),
                                           top[:, :, 1, :].unsqueeze(2).to_broadcast([P, HEADS, TOPK, TOPK]), ALU.add))
                    dve.tensor_copy(topf.rearrange("p h c k -> p (h c k)"), topi)
                    c2 = cand.rearrange("p (h a) -> p h a", h=HEADS)
                    a2 = alt.rearrange("p (h a) -> p h a", h=HEADS)
                    s2 = sel.rearrange("p (h k) -> p h k", h=HEADS)
                    i2 = seli.rearrange("p (h k) -> p h k", h=HEADS)
                    top16([c2[:, h, :] for h in range(HEADS)], [a2[:, h, :] for h in range(HEADS)],
                          [s2[:, h, :] for h in range(HEADS)], [i2[:, h, :] for h in range(HEADS)], HEADS, 256)
                    dve.tensor_copy(gsum[:, 0:HEADS], s2[:, :, 0])
                    link(dve.tensor_scalar(hi, seli, 4, None, ALU.logical_shift_right))
                    dve.tensor_tensor(s2, s2, gsum[:, 0:HEADS].unsqueeze(2).to_broadcast([P, HEADS, TOPK]),
                                      ALU.subtract).then_inc(sub_ready, 1)
                    link(dve.tensor_scalar(seli, seli, 15, None, ALU.bitwise_and))
                    dve.tensor_copy(route[:, 0, :], hi)
                    link(dve.tensor_copy(route[:, 1, :], seli))
                    for half, buf in ((0, alt), (1, cand)):
                        eq = buf.rearrange("p (s a) -> p s a", a=TOPK)
                        dve.tensor_tensor(eq, route[:, half, :].unsqueeze(2).to_broadcast([P, P, TOPK]),
                                          con("iota16").unsqueeze(1).to_broadcast([P, P, TOPK]), ALU.is_equal)
                    link(dve.tensor_copy(gsum[:, HEADS:], gsum[:, 0:HEADS]))
                    for half, buf in ((0, alt), (1, cand)):
                        eq = buf.rearrange("p (h s a) -> p h s a", h=HEADS, a=TOPK)
                        last = dve.tensor_tensor(eq, eq, topf[:, :, half, :].unsqueeze(2).to_broadcast(
                            [P, HEADS, TOPK, TOPK]), ALU.mult)
                    link(last)
                    for half, buf in ((0, alt), (1, cand)):
                        dve.tensor_reduce(route[:, half, :], buf.rearrange("p (s a) -> p s a", a=TOPK), AX_X, ALU.add)
                    dve.wait_ge(gexp_ready, tile + 1)
                    link(dve.tensor_reduce(gsum[:, 0:HEADS], s2, AX_X, ALU.add))
                    link(dve.reciprocal(gsum[:, 0:HEADS], gsum[:, 0:HEADS]))
                    dve.tensor_tensor(route[:, 2, :].rearrange("p (h k) -> p h k", h=HEADS), s2,
                                      gsum[:, 0:HEADS].unsqueeze(2).to_broadcast([P, HEADS, TOPK]),
                                      ALU.mult).then_inc(route_ready, 1)
                    dve.wait_ge(route_in, tile + 1)

                    with dve.Fori(0, 2) as i:
                        for s4 in range(GTURNS // 2):
                            for q in range(GB):
                                dve.wait_ge(g_mm[q], i * (GTURNS // 2) + (GTURNS * tile + s4 + 1))
                                for k in range(4):
                                    s = 4 * q + k
                                    tok = i * (P // 2) + (s4 * GTOK + s)
                                    dve.tensor_scalar(oneh1[:, s, :], con("iota"), routeT[:, 0, bass.ds(tok, 1)],
                                                      None, ALU.is_equal)
                                    last = dve.tensor_scalar(oneh2[:, s, :], con("iota"),
                                                             routeT[:, 1, bass.ds(tok, 1)],
                                                             routeT[:, 2, bass.ds(tok, 1)], ALU.is_equal, ALU.mult)
                                last.then_inc(onehot, 1)

            def output_pass(l):
                n0 = BLOCK["ex", l, NU]
                base = NGROUP * GJ * l

                def gated(g, j, b, turn):
                    if j == 0:
                        dve.wait_ge(g_landed[b], turn * 32 + 32 * (NGROUP // 2 * l + 1))
                    dve.tensor_tensor(hid[b][:, j, :], hid[b][:, j, :], gate[b][:, j, :],
                                      ALU.mult).then_inc(hid_ready, 1)

                def step(g, b, turn):
                    for c in range(KC):
                        gated(g + 1, c, 1 - b, turn)
                        dve.wait_ge(block_done, g * GJ + (n0 + c + 1))
                        residual(pair[2 + c % 2], c, l, 5 * KC).then_inc(y_added, 1)

                for j in range(GJ):
                    gated(0, j, 0, 0)
                dve.wait_ge(x_in, 16 * (l + 1))
                step(0, 0, 0)
                with dve.Fori(0, (NGROUP - 2) // 2) as i:
                    step(i * 2 + 1, 1, i + 1)
                    step(i * 2 + 2, 0, i + 1)
                for c in range(KC):
                    dve.wait_ge(block_done, n0 + (NGROUP - 1) * GJ + c + 1)
                    residual(pair[2 + c % 2], c, l, 5 * KC).then_inc(y_added, 1)

            modulation(0, 0, FIRST_MOD, BLOCK["mod", 0, FIRST_MOD - 1])
            for l in range(L):
                norm(2 * l)
                posts(l)
                attention(l)
                out_projection(l)
                norm(2 * l + 1)
                gates(l)
                output_pass(l)
            norm(2 * L)

        @block.gpsimd
        def _(pool):
            pool.wait_ge(inputs_in, 16 * N_INPUTS)
            for l in range(L):
                if l:
                    pool.wait_ge(y_added, NGROUP * KC * l)
                pool.dma_start(table, a["tables"]).then_inc(layer_in, 16)
                pool.dma_start(kc, a["cache_kT"][l]).then_inc(layer_in, 16)
                pool.dma_start(vc, a["cache_v"][l]).then_inc(layer_in, 16)
                for par in range(2):
                    pool.dma_start(bias[64 * par:64 * par + 64],
                                   a["rpb"][l, :, :, 1 - par:1 - par + BROWS, :]).then_inc(bias_in, 16)
                pool.wait_ge(bias_in, 16 * 2 * (l + 1))
                for h in range(6):
                    pool.tensor_tensor(bias[:, h], bias[:, h], con("mask").unsqueeze(1).to_broadcast([P, BROWS, 64]),
                                       ALU.add).then_inc(bias_ready, 1)
                pool.wait_ge(proj_evac, PROJ * l + NWIN)
                pool.wait_ge(post_fin, POSTS * l + 4)
                for j, (ch, n) in enumerate(((CK, 1), (BK, 2), (AK, 3))):
                    pool.dma_start(a["out_kT"][l, :, (0, 1, 3)[j]:(0, 1, 3)[j] + n],
                                   qk[:, ch:ch + n, NLAT:TOK]).then_inc(kv_stored, 16)
                pool.dma_start(a["out_v"][l], vN[:, TT - 1, :]).then_inc(kv_stored, 16)
                pool.wait_ge(lam_ready, L)
                for n in range(NMAP):
                    if n in SCALED:
                        m = MAPS[n]
                        w = TOK if m["t"] < TT - 1 else NCTX
                        s = n % 4
                        pool.wait_ge(rinv_done, NMAP * l + n + 1)
                        pool.tensor_scalar(prob[:, s, 0:w], prob[:, s, 0:w], stat[:, 8 + s:9 + s],
                                           nlam[:, l:l + 1] if m["kind"] == "B" else 1.0,
                                           ALU.mult, ALU.mult).then_inc(scaled, 1)
                pool.wait_ge(kv_stored, 16 * 4 * (l + 1))
                pool.wait_ge(h_ready, 2 * l + 2)
                pool.dma_start(keys, a["keysT"][l]).then_inc(keys_in, 16)


def constants():
    p = np.arange(P)
    c = {}
    c["ident"] = np.eye(P)
    c["ones"] = np.ones((P, P))
    c["pairsum"] = (p[:, None] // 64 == p[None, :] // 64)
    for name, n in (("rotB", 8), ("rotC", 16)):
        m = np.zeros((P, P))
        for d in range(P):
            if d % (2 * n) < n:
                m[d + n, d] = -1.0
            else:
                m[d - n, d] = 1.0
        c[name] = m
    c["iota"] = np.tile(np.arange(P), (P, 1))
    c["iota16"] = np.tile(np.arange(16), (P, 1))
    qc = p[:, None] % GRID_W
    kcol = np.arange(GRID_W)[None, :]
    lo = np.clip(qc - 8, 0, GRID_W - 16)
    c["mask"] = np.where((kcol >= lo) & (kcol < lo + 16), 0.0, NEG)
    tok = np.arange(NLAT)
    t = {}
    for name, dim in (("C", 64), ("B", 32)):
        q = dim // 4
        d = p % dim
        inv = (np.float32(10000.0) ** (-(np.arange(q, dtype=np.float32)) / np.float32(q))).astype(np.float32)
        pos = np.where((d // (dim // 2) == 0)[:, None], (tok // GRID_W)[None, :], (tok % GRID_W)[None, :])
        ang = pos.astype(np.float32) * inv[d % q][:, None]
        t["cos" + name] = np.cos(ang)
        t["sin" + name] = np.sin(ang)
    cat = lambda parts, src: np.concatenate([src[n] for n, _ in parts], 1).astype(np.float32)
    return cat(CONSTS, c), cat(TABLES, t)


def blocks(w):
    K, M = w.shape
    return w.reshape(K // P, P, M // P, P).transpose(2, 1, 0, 3)


def chunked(v):
    v = v.reshape(*v.shape[:-1], -1, P)
    return np.moveaxis(v, -1, 0)


C_PAIRS = [0, 3, 1, 4, 2, 5]


def kernel(x_prompt, x_sample, cache_a_k, cache_a_v, cache_b_k, cache_b_v, cache_c_k, cache_c_v, c, c_ctx,
           w_mod, b_mod, norm_g, w_in, w_out, na_rpb, diff_lambda, diff_subln, gqa_qk_norm, peer_wq,
           peer_keys, peer_u, peer_v, final_g):
    import concourse.bacc as bacc
    from concourse.bass_utils import run_bass_kernel_spmd

    ins = {}
    x = np.concatenate([x_sample.reshape(NLAT, D), x_prompt.reshape(NCTX, D)], 0)
    ins["xT"] = x.T.reshape(KC, P, TOK).transpose(1, 0, 2)
    ins["cT"] = np.stack([c.reshape(KC, P).T, c_ctx.reshape(KC, P).T], 2)
    ins["const"], ins["tables"] = constants()
    ins["cols"] = np.concatenate([
        chunked(b_mod).reshape(P, -1), chunked(norm_g).reshape(P, -1), chunked(final_g).reshape(P, -1),
        np.concatenate([gqa_qk_norm, gqa_qk_norm], -1).reshape(L * 2, P).T,
        np.concatenate([diff_subln, diff_subln], -1).T], 1)
    ins["lam"] = diff_lambda
    ins["w_mod"] = np.stack([blocks(w_mod[l]) for l in range(L)])
    edge = np.cumsum([0, 384, 384, 384, 256, 256, 256, 384, 128, 128])
    part = [np.arange(edge[i], edge[i + 1]) for i in range(9)]
    pairs = np.concatenate([np.arange(64 * h, 64 * h + 64) for h in C_PAIRS])
    order = np.concatenate([part[6][pairs], part[7], part[3], part[4], part[0], part[1], part[2], part[5], part[8]])
    ins["w_in"] = np.stack([blocks(w_in[l][:, order]) for l in range(L)])
    rows = np.concatenate([np.arange(640), 640 + pairs])
    ins["w_out"] = np.stack([blocks(w_out[l][rows]) for l in range(L)])
    ins["w_query"] = np.stack([blocks(peer_wq[l]) for l in range(L)])
    ins["keysT"] = peer_keys.reshape(L, HC, NK, P).transpose(0, 3, 1, 2)
    u = peer_u.reshape(L, P, NGROUP, GJ, KC, P).transpose(0, 2, 3, 5, 4, 1)
    v = peer_v.reshape(L, P, NGROUP, GJ, KC, P).transpose(0, 2, 4, 1, 3, 5)
    ex = np.empty((L, 2 * NGROUP * GJ, P, KC, P), u.dtype)
    seq = [("u", g) for g in range(NGROUP)] + [("v", g) for g in range(NGROUP)]
    for n, (kind, g) in enumerate(seq):
        ex[:, n * GJ:(n + 1) * GJ] = (u if kind == "u" else v)[:, g]
    ins["expert"] = ex
    rpb = np.zeros((L, 6, 15, 127), na_rpb.dtype)
    rpb[..., 63 - 15:63 + 16] = na_rpb
    ins["rpb"] = np.stack([rpb[..., 63 - q:127 - q] for q in range(GRID_W)], 1)
    ck = np.concatenate([cache_c_k.reshape(L, NCTX, P), cache_b_k.reshape(L, NCTX, 2 * P),
                         cache_a_k.reshape(L, NCTX, 3 * P)], 2)
    ins["cache_kT"] = ck.reshape(L, NCTX, 6, P).transpose(0, 3, 2, 1)
    ins["cache_v"] = np.concatenate([cache_a_v.reshape(L, NCTX, -1), cache_b_v.reshape(L, NCTX, -1),
                                     cache_c_v.reshape(L, NCTX, -1)], 2)
    outs = {"out_yT": (P, KC, TOK), "out_kT": (L, P, 6, NCTX), "out_v": (L, NCTX, VW)}

    nc = bacc.Bacc("TRN2", target_bir_lowering=False, num_devices=1)
    arrays, args = {}, {}
    for name, v_ in ins.items():
        arrays[name + "_dram"] = np.ascontiguousarray(v_)
        args[name] = nc.dram_tensor(name + "_dram", v_.shape, F32, kind="ExternalInput").ap()
    for name, shape in outs.items():
        args[name] = nc.dram_tensor(name, shape, F32, kind="ExternalOutput").ap()
    build(nc, args)
    r = run_bass_kernel_spmd(nc, [arrays], core_ids=[0]).results[0]
    y = r["out_yT"].transpose(2, 1, 0).reshape(TOK, D)
    kT = r["out_kT"].transpose(0, 3, 2, 1).reshape(L, NCTX, 6 * P)
    v = r["out_v"]
    return (y[NLAT:].reshape(1, NCTX, D), y[:NLAT].reshape(1, NLAT, D),
            kT[..., 384:].reshape(1, L, NCTX, 6, 64), v[..., 0:384].reshape(1, L, NCTX, 6, 64),
            kT[..., 128:384].reshape(1, L, NCTX, 4, 2, 32), v[..., 384:640].reshape(1, L, NCTX, 4, 64),
            kT[..., 0:128].reshape(1, L, NCTX, 2, 64), v[..., 640:].reshape(1, L, NCTX, 2, 64))
```

```python
import math
from contextlib import ExitStack

import numpy as np

import concourse.bass as bass
from concourse import mybir

F32 = mybir.dt.float32
U32 = mybir.dt.uint32
F16 = mybir.dt.float16
ALU = mybir.AluOpType
ACT = mybir.ActivationFunctionType
AX_X = mybir.AxisListType.X

P = 128
D = 1024
KC = D // P
L = 2
NLAT, NCTX = 512, 128
TOK = NLAT + NCTX
TT = TOK // P
GRID_W, ROWS = 64, NLAT // 64
EPS = 1e-6
NEG = -1.0e30
LOWEST = -3.0e38
CQ, CK, BQ, BK, AQ, AK = 0, 3, 4, 6, 8, 11
NQK = 14
VW = 768
NV = VW // P
NWIN = NQK + NV
B_SCALE = 32.0 ** -0.5
BROWS = 14
HEADS, TOPK, NK = 8, 16, 128
HC = 2 * HEADS
NGROUP, GJ = 16, 8
NU = NGROUP * GJ
UA = 16
EXP_AFTER = 11
NMOD = 48
RING = 4
HSLOT = 4
EXPONENT = 0x7F800000
TOP = 14
TINY = 2.0 ** -100
POSTS = 12
GTOK, GB = 16, 4
GTURNS = P // GTOK
OCHUNKS = (0, 1, 2, 5, 6, 7, 3, 4)
NDESC = NWIN + HC + NU
NRES = KC + NGROUP * KC
OPAIR = (2, 1)
NPROB = 6
LAG_T, LAG_V = 3, 4
GLINKS = 7

CONSTS = [("ident", 128), ("ones", 128), ("pairsum", 128), ("rotB", 128), ("rotC", 128),
          ("iota", 128), ("iota16", 16), ("mask", 64)]
TABLES = [("cosC", 512), ("sinC", 512), ("cosB", 512), ("sinB", 512)]
COLS = [("bmod", L * NMOD), ("gain", L * 2 * KC), ("fgain", KC), ("qkgain", L * 2), ("subln", L)]


def offsets(parts):
    out, at = {}, 0
    for name, n in parts:
        out[name] = at
        at += n
    return out, at


CO, NCONST = offsets(CONSTS)
TO, NTABLE = offsets(TABLES)
FO, NCOLS = offsets(COLS)


def attention_plan():
    maps, items, units = [], [], []
    for kind, chunks in (("A", 3), ("B", 2), ("C", 3)):
        for ch in range(chunks):
            for t in range(TT):
                for hh in range(2):
                    per = 2 if kind == "B" else 1
                    for c in range(per):
                        if kind == "A":
                            q, k, kp, kn, cc = AQ + ch, AK + ch, 64 * hh, 64, 3 + ch
                        elif kind == "B":
                            m = 2 * (2 * ch + hh) + c
                            q, k, kp, kn, cc = BQ + m // 4, BK + m // 4, 32 * (m % 4), 32, 1 + m // 4
                        else:
                            q, k, kp, kn, cc = CQ + ch, CK, 64 * hh, 64, 0
                        maps.append(dict(kind=kind, q=q, k=k, kp=kp, kn=kn, cc=cc, t=t, c=c,
                                         head=2 * ch + hh, item=len(items)))
                    vcol = {"A": 64 * (2 * ch + hh), "B": 384 + 64 * (2 * ch + hh), "C": 640 + 64 * hh}[kind]
                    items.append(dict(kind=kind, t=t, hh=hh, vcol=vcol, last=len(maps) - 1,
                                      first=len(maps) - per, unit=len(units)))
                units.append(dict(t=t, chunk={"A": 0, "B": 3, "C": 5}[kind] + ch, last=len(items) - 1))
    return maps, items, units


MAPS, ITEMS, UNITS = attention_plan()
NMAP, NITEM, NUNIT = len(MAPS), len(ITEMS), len(UNITS)
BY_LAST = {it["last"]: i for i, it in enumerate(ITEMS)}
UNIT_BY_LAST = {ITEMS[u["last"]]["last"]: i for i, u in enumerate(UNITS)}
SCALED = {m: i for i, m in enumerate([m for m, x in enumerate(MAPS) if x["kind"] != "B" or x["c"] == 1])}
MIXED = {i: n for n, i in enumerate([i for i, x in enumerate(ITEMS) if x["kind"] == "B"])}
NSCALED, NMIXED = len(SCALED), len(MIXED)

FIRST_MOD = 16
MOD_IN = [[(l, m) for m in range(FIRST_MOD, NMOD)] + [(l + 1, m) for m in range(FIRST_MOD) if l + 1 < L]
          for l in range(L)]


def block_plan():
    plan = [("mod", 0, m) for m in range(FIRST_MOD)]
    for l in range(L):
        plan += [("win", l, i) for i in range(NWIN)]
        plan += [("mod", a, m) for a, m in MOD_IN[l]]
        plan += [("wout", l, i) for i in range(KC)]
        plan += [("wq", l, i) for i in range(HC)]
        plan += [("ex", l, i) for i in range(NGROUP * 2 * GJ)]
    return {key: n for n, key in enumerate(plan)}


BLOCK = block_plan()
ORDER = list(BLOCK)
SPLIT = {key: i for i, key in enumerate(k for k in ORDER if k[0] != "mod")}
MODS = {key: i for i, key in enumerate(k for k in ORDER if k[0] == "mod")}
SEGMENTS = [(SPLIT["win", 0, 0], SPLIT["win", 0, NWIN - 1]), (SPLIT["wout", 0, 0], SPLIT["win", 1, NWIN - 1]),
            (SPLIT["wout", 1, 0], SPLIT["ex", 1, 2 * NU - 1])]
SPLIT_KEYS = list(SPLIT)


def segment(b):
    return next(x for x in SEGMENTS if x[0] <= b <= x[1])


def ahead(k, seg):
    return seg[0] <= k <= seg[1]


def build(nc, a):
    with ExitStack() as ctx:
        def sb(name, shape, dt=F32):
            return ctx.enter_context(nc.sbuf_tensor(name, shape, dt))

        def sem(name):
            return ctx.enter_context(nc.semaphore(name))

        xT = sb("xT", [P, KC, TOK])
        hT = sb("hT", [P, KC, TOK])
        oT = hT
        hHL = hT[:].rearrange("p c t -> p (c t)").bitcast(F16).rearrange("p (s c t) -> p s c t", s=2, c=KC)
        ring = sb("ring", [P, RING, KC, P])
        split = sb("split", [P, RING, 2, KC, P], F16)
        bmax = sb("bmax", [P, RING])
        ball = sb("ball", [P, RING])
        bpow = sb("bpow", [P, RING])
        bscale = sb("bscale", [P, RING])
        descale = sb("descale", [P, RING])
        xstat = sb("xstat", [P, 8])
        xpow, xscale, xinv = sb("xpow", [P, 1]), sb("xscale", [P, 1]), sb("xinv", [P, 1])
        vpow, vscale, vinv = sb("vpow", [P, 1]), sb("vscale", [P, 1]), sb("vinv", [P, 1])
        hpow, hscale, hinv = sb("hpow", [P, 2]), sb("hscale", [P, 2]), sb("hinv", [P, 2])
        hmax = sb("hmax", [P, 4])
        gmax, gall = sb("gmax", [P, 1]), sb("gall", [P, 1])
        tiny = sb("tiny", [P, 1])
        xall = sb("xall", [P, 1])
        affine = sb("affine", [P, 2, KC, 2])
        gatecol = sb("gatecol", [P, 2, 2])
        const = sb("const", [P, NCONST])
        cols = sb("cols", [P, NCOLS])
        modT = sb("modT", [P, L, NMOD, 2])
        cT = sb("cT", [P, KC, 2])
        cexp = sb("cexp", [P, KC, 2])
        lam = sb("lam", [P, L, 4, 32])
        lprod = sb("lprod", [P, L, 2, 32])
        lsum = sb("lsum", [P, L, 2])
        nlam = sb("nlam", [P, L])
        stat = sb("stat", [P, 3, NPROB])
        WORK = 32900
        work = sb("work", [P, WORK])

        def at(off, *shape):
            n = int(np.prod(shape))
            assert off + n <= WORK
            ap = work[:, off:off + n]
            names = "abcd"[:len(shape)]
            if len(shape) > 1:
                ap = ap.rearrange(f"p ({' '.join(names)}) -> p {' '.join(names)}",
                                  **{x: s for x, s in zip(names, shape)})
            return ap

        qk = at(0, NQK, TOK)
        o = NQK * TOK
        vN = at(o, TT, VW); o += TT * VW
        kc = at(o, 6, P); o += 6 * P
        vc = at(o, VW); o += VW
        bias = at(o, 6, BROWS, GRID_W); o += 6 * BROWS * GRID_W
        table = at(o, NTABLE); o += NTABLE
        y32 = at(o, KC, TOK)
        oHL = at(o, KC * TOK).bitcast(F16).rearrange("p (s c t) -> p s c t", s=2, c=KC)
        o_end = o + KC * TOK
        prob = at(o, NPROB, TOK); o += NPROB * TOK
        probT = at(o, 2, TOK); o = o_end
        sq = at(o, 2, TOK); o += 2 * TOK
        var = at(o, TOK); o += TOK
        rs = at(o, TOK); o += TOK
        scores = at(0, TT, HC, P)
        o = TT * HC * P
        alt = at(o, HC * P); cand = at(o + HC * P, HC * P); o += 2 * HC * P
        gst = at(o, P, P)
        keys = at(o, HC, P)
        qTb = at(o + HC * P, 2, TOK)
        o += P * P
        top = at(o, HEADS, 2, TOPK); o += 256
        topi = at(o, HEADS * 2 * TOPK).bitcast(U32); o += 256
        topf = at(o, HEADS, 2, TOPK); o += 256
        sel = at(o, P); o += P
        seli = at(o, P).bitcast(U32); o += P
        hi = at(o, P).bitcast(U32); o += P
        route = at(o, 3, P); o += 3 * P
        routeT = at(o, 3, P); o += 3 * P
        gsum = at(o, 2 * HEADS); o += 2 * HEADS
        oneh1 = alt.rearrange("p (t i) -> p t i", i=P)
        oneh2 = cand.rearrange("p (t i) -> p t i", i=P)
        hid = [at(i * GJ * TOK, GJ, TOK) for i in range(2)]
        gate = [at((2 + i) * GJ * TOK, GJ, TOK) for i in range(2)]
        hidHL = [at((4 + i) * GJ * TOK, GJ * TOK).bitcast(F16).rearrange("p (s j t) -> p s j t", s=2, j=GJ)
                 for i in range(2)]

        psum = ctx.enter_context(nc.psum_tensor("psum", [P, 8, 512], F32))
        pair = [psum[:, 2 * i:2 * i + 2, :].rearrange("p b n -> p (b n)") for i in range(4)]
        modps = psum[:, 7, 0:L * NMOD * 2].rearrange("p (l m s) -> p l m s", l=L, s=2)

        def con(name, p=P):
            return const[0:p, CO[name]:CO[name] + dict(CONSTS)[name]]

        def tab(name):
            return table[:, TO[name]:TO[name] + 512]

        def col(name, i):
            return cols[:, FO[name] + i:FO[name] + i + 1]

        gdram = nc.dram_tensor("gate_matrix", (P, P, TOK), F32, kind="Internal").ap()

        hdram = nc.dram_tensor("hidden", (P, P, TOK), F32, kind="Internal").ap()
        xdram = nc.dram_tensor("residual", (P, KC, TOK), F32, kind="Internal").ap()

        inputs_in = sem("inputs_in")
        residual_in = sem("residual_in")
        landed = [sem(f"landed{i}") for i in range(RING)]
        mod_used = sem("mod_used")
        bmax_done = sem("bmax_done")
        ball_done = sem("ball_done")
        scale_done = sem("scale_done")
        high_done = sem("high_done")
        split_done = sem("split_done")
        used = sem("used")
        descale_done = sem("descale_done")
        xmax_done = sem("xmax_done")
        xall_done = sem("xall_done")
        xhigh_in = sem("xhigh_in")
        xhigh_done = sem("xhigh_done")
        oscale_done = sem("oscale_done")
        ohigh_done = sem("ohigh_done")
        olow_done = sem("olow_done")
        bpow_done = sem("bpow_done")
        gate_set = sem("gate_set")
        group_chain = sem("group_chain")
        gmax_done = sem("gmax_done")
        gall_done = sem("gall_done")
        asked = sem("asked")
        tiny_set = sem("tiny_set")
        block_reduced = sem("block_reduced")
        x_reduced = sem("x_reduced")
        g_reduced = sem("g_reduced")
        hscale_done = sem("hscale_done")
        hhigh_done = sem("hhigh_done")
        c_sq = sem("c_sq")
        b_sq = sem("b_sq")
        dve_chain = sem("dve_chain")
        silu_exp = sem("silu_exp")
        c_ready = sem("c_ready")
        lam_sum = sem("lam_sum")
        lam_exp = sem("lam_exp")
        lam_ready = sem("lam_ready")
        mod_ready = sem("mod_ready")
        sq_ready = sem("sq_ready")
        sum_step = sem("sum_step")
        var_ready = sem("var_ready")
        sd_ready = sem("sd_ready")
        hlow_done = sem("hlow_done")
        proj_evac = sem("proj_evac")
        post_mm = sem("post_mm")
        post_fin = sem("post_fin")
        layer_in = sem("layer_in")
        bias_in = sem("bias_in")
        bias_ready = sem("bias_ready")
        kv_stored = sem("kv_stored")
        score_done = sem("score_done")
        max_done = sem("max_done")
        exp_done = sem("exp_done")
        rinv_done = sem("rinv_done")
        scaled = sem("scaled")
        mixed = sem("mixed")
        tr_done = sem("tr_done")
        pt_done = sem("pt_done")
        pv_done = sem("pv_done")
        o_evac = sem("o_evac")
        bn_mm = sem("bn_mm")
        bn_fin = sem("bn_fin")
        wout_added = sem("wout_added")
        keys_in = sem("keys_in")
        keyscore = sem("keyscore")
        scores_in = sem("scores_in")
        sub_ready = sem("sub_ready")
        gexp_ready = sem("gexp_ready")
        route_ready = sem("route_ready")
        route_tr = sem("route_tr")
        route_in = sem("route_in")
        onehot = sem("onehot")
        g_mm = [sem(f"g_mm{q}") for q in range(GB)]
        g_evac = [sem(f"g_evac{q}") for q in range(GB)]
        g_stored = sem("g_stored")
        hid_out = [sem(f"hid_out{i}") for i in range(HSLOT)]
        x_out = sem("x_out")
        x_in = sem("x_in")
        g_landed = [sem(f"g_landed{i}") for i in range(2)]
        gelu_done = sem("gelu_done")
        hid_ready = sem("hid_ready")
        y_added = sem("y_added")
        y_ready = sem("y_ready")
        y_stored = sem("y_stored")

        PROJ = NWIN + HC
        NORMS = 2 * L + 1
        ROOTS = 2 + 4 + 2

        def roots(l, i):
            return l * ROOTS + i + 1

        N_INPUTS = 4
        block = ctx.enter_context(nc.Block())

        @block.sync
        def _(sp):
            for dst, src in ((cT[:], a["cT"]), (const[:], a["const"]), (cols[:], a["cols"]),
                             (lam[:], a["lam"].partition_broadcast(P))):
                sp.dma_start(dst, src).then_inc(inputs_in, 16)

            def load(key, src):
                n = BLOCK[key]
                if n >= RING:
                    before = ORDER[n - RING]
                    if before[0] == "mod":
                        sp.wait_ge(mod_used, MODS[before] + 1)
                    else:
                        sp.wait_ge(split_done, SPLIT[before] + 1)
                sp.dma_start(ring[:, n % RING], src).then_inc(landed[n % RING], 16)

            def hidden_pass(l):
                n0, b0 = BLOCK["ex", l, 0], SPLIT["ex", l, 0]
                src = a["expert"][l]

                def store(i, k):
                    sp.wait_ge(gelu_done, i * GJ + (NU * l + k + 1))
                    sp.dma_start(hdram[bass.ds(i * GJ + k, 1)].rearrange("o i t -> i (o t)"),
                                 xT[:, k % HSLOT, :]).then_inc(hid_out[k % HSLOT], 16)

                for k in range(GJ):
                    load(("ex", l, k), src[k])
                    if k == 2:
                        sp.wait_ge(hlow_done, KC * (2 * l + 2))
                        sp.dma_start(xdram, xT[:]).then_inc(x_out, 16)
                with sp.Fori(1, NGROUP) as i:
                    for k in range(GJ):
                        n = n0 + k
                        sp.wait_ge(split_done, i * GJ + (b0 + k - RING + 1))
                        sp.dma_start(ring[:, n % RING], src[i * GJ + k]).then_inc(landed[n % RING], 16)
                        store(i - 1, k)
                return store

            def output_pass(l, store):
                n0, b0 = BLOCK["ex", l, NU], SPLIT["ex", l, NU]
                src = a["expert"][l]

                def inputs(g, b, part):
                    if part == 0:
                        for k in range(HSLOT):
                            sp.wait_ge(hid_out[k], g * 32 + 32 * (NGROUP * l + 1))
                    js = slice(GJ // 2 * (part // 2), GJ // 2 * (part // 2 + 1))
                    dst, src_ = (gate[b], gdram) if part % 2 else (hid[b], hdram)
                    sp.dma_start(dst[:, js, :], src_.rearrange("(g j) i t -> g i j t", j=GJ)[g][:, js, :]
                                 ).then_inc(g_landed[b], 16)

                for k in range(RING):
                    load(("ex", l, NU + k), src[NU + k])
                    store(NGROUP - 1, k)
                    if k == 1:
                        sp.wait_ge(g_stored, 16 * TT * (l + 1))
                        for part in range(4):
                            inputs(0, 0, part)
                for part in range(4):
                    inputs(1, 1, part)
                for k in range(RING, GJ):
                    store(NGROUP - 1, k)
                for k in range(HSLOT):
                    sp.wait_ge(hid_out[k], 32 * NGROUP * (l + 1))
                sp.dma_start(xT[:], xdram).then_inc(x_in, 16)
                for k in range(RING, GJ):
                    load(("ex", l, NU + k), src[NU + k])

                def step(g, b):
                    for k in range(GJ):
                        n = n0 + k
                        sp.wait_ge(split_done, g * GJ + (b0 + k - RING + 1))
                        sp.dma_start(ring[:, n % RING], src[NU + g * GJ + k]).then_inc(landed[n % RING], 16)
                        if k == 0:
                            sp.wait_ge(hid_ready, (g - 1) * 2 + (2 * NGROUP * l + 2))
                        if k < 4:
                            inputs(g + 1, 1 - b, k)

                with sp.Fori(0, (NGROUP - 2) // 2) as i:
                    step(i * 2 + 1, 1)
                    step(i * 2 + 2, 0)
                for k in range(GJ):
                    load(("ex", l, NU + (NGROUP - 1) * GJ + k), src[NU + (NGROUP - 1) * GJ + k])

            for m in range(FIRST_MOD):
                load(("mod", 0, m), a["w_mod"][0, m])
            sp.dma_start(xT[:], a["xT"]).then_inc(residual_in, 16)
            for l in range(L):
                for i in range(NWIN):
                    load(("win", l, i), a["w_in"][l, i])
                for b, m in MOD_IN[l]:
                    load(("mod", b, m), a["w_mod"][b, m])
                for i in range(KC):
                    load(("wout", l, i), a["w_out"][l, i])
                for i in range(HC):
                    load(("wq", l, i), a["w_query"][l, i])
                output_pass(l, hidden_pass(l))
            sp.wait_ge(y_ready, 1)
            sp.dma_start(a["out_yT"], hT[:]).then_inc(y_stored, 16)
            sp.wait_ge(y_stored, 16)
            sp.wait_ge(kv_stored, 16 * 4 * L)

        @block.tensor
        def _(pe):
            def take(b):
                pe.wait_ge(split_done, b + 1)
                return split[:, b % RING]

            def wide(out, lhsT_of, rhs_of, ks, width=TOK):
                for lo, hi_ in ((0, 512), (512, width)):
                    if lo >= hi_:
                        continue
                    for k in range(ks):
                        last = pe.matmul(out[:, lo:hi_], lhsT_of(k), rhs_of(k)[:, lo:hi_],
                                         start=(k == 0), stop=(k == ks - 1))
                return last

            PASSES = ((0, 0), (0, 1), (1, 0))

            def wide3(out, w, x, order=range(KC), ready=None, count=0):
                for lo, hi_ in ((0, 512), (512, TOK)):
                    for s, k in enumerate(order):
                        if ready is not None and lo == 0:
                            pe.wait_ge(ready, count + s + 1)
                        for n, (i, j) in enumerate(PASSES):
                            last = pe.matmul(out[:, lo:hi_], w[:, i, k, :], x[:, j, k, lo:hi_],
                                             start=(s == 0 and n == 0), stop=(s == KC - 1 and n == 2))
                return last

            def mod_block(l, m):
                n = BLOCK["mod", l, m]
                pe.wait_ge(landed[n % RING], 16 * (n // RING + 1))
                w = ring[:, n % RING]
                for k in range(KC):
                    last = pe.matmul(modps[:, l, m, :], w[:, k, :], cT[:, k, :], start=(k == 0), stop=(k == KC - 1))
                last.then_inc(mod_used, 1)

            def norm(ni):
                for c in range(KC):
                    pe.wait_ge(sq_ready, KC * ni + c + 1)
                    for lo, hi_ in ((0, 512), (512, TOK)):
                        last = pe.matmul(pair[0][:, lo:hi_], con("ones"), sq[:, c % 2, lo:hi_],
                                         start=(c == 0), stop=(c == KC - 1))
                    last.then_inc(sum_step, 1)

            def post(l, p):
                if POSTS * l + p > 0:
                    pe.wait_ge(post_fin, POSTS * l + p)
                if p < 4:
                    pe.wait_ge(c_sq, 4 * l + p + 1)
                    wide(pair[2], lambda k: con("pairsum"), lambda k: sq[:, p % 2, :], 1).then_inc(post_mm, 1)
                else:
                    ch = p - 4
                    pe.wait_ge(proj_evac, PROJ * l + ch + 1)
                    rot = con("rotC" if ch < BQ else "rotB")
                    pe.matmul(pair[2][:, 0:NLAT], rot, qk[:, ch, 0:NLAT], start=True, stop=True).then_inc(post_mm, 1)

            def project(l):
                for i in range(NWIN):
                    if i >= 2:
                        pe.wait_ge(proj_evac, PROJ * l + i - 1)
                    w = take(SPLIT["win", l, i])
                    out = pair[i % 2]
                    if i < NQK:
                        last = wide3(out, w, hHL, ready=None if i else hlow_done, count=KC * 2 * l)
                    else:
                        for t in range(TT):
                            for k in range(KC):
                                for n, (x_, w_) in enumerate(PASSES):
                                    last = pe.matmul(out[:, t * P:(t + 1) * P], hHL[:, x_, k, t * P:(t + 1) * P],
                                                     w[:, w_, k, :], start=(k == 0 and n == 0),
                                                     stop=(k == KC - 1 and n == 2))
                    last.then_inc(used, 1)
                    if 4 <= i < 4 + POSTS:
                        post(l, i - 4)

            def attention(l):
                pe.wait_ge(proj_evac, PROJ * l + NWIN)
                pe.wait_ge(post_fin, POSTS * (l + 1))
                pe.wait_ge(layer_in, 16 * 3 * (l + 1))
                extra = list(MOD_IN[l])
                for n in range(NMAP + LAG_V):
                    if n < NMAP:
                        m = MAPS[n]
                        ps = pair[n % 2]
                        if n >= 2:
                            pe.wait_ge(exp_done, NMAP * l + n - 1)
                        kp, kn, t = m["kp"], m["kn"], m["t"]
                        q = qk[kp:kp + kn, m["q"], t * P:(t + 1) * P]
                        if t < TT - 1:
                            pe.matmul(ps[:, 0:NLAT], q, qk[kp:kp + kn, m["k"], 0:NLAT], start=True, stop=True)
                            last = pe.matmul(ps[:, NLAT:TOK], q, kc[kp:kp + kn, m["cc"], :], start=True, stop=True)
                        else:
                            last = pe.matmul(ps[:, 0:NCTX], q, qk[kp:kp + kn, m["k"], NLAT:TOK], start=True, stop=True)
                        last.then_inc(score_done, 1)
                        if n % 2 == 0 and extra:
                            mod_block(*extra.pop(0))
                    if n - LAG_T in BY_LAST:
                        i = BY_LAST[n - LAG_T]
                        it = ITEMS[i]
                        if it["kind"] == "B":
                            pe.wait_ge(mixed, NMIXED * l + MIXED[i] + 1)
                        else:
                            pe.wait_ge(scaled, NSCALED * l + SCALED[n - LAG_T] + 1)
                        if i > 0:
                            pe.wait_ge(pt_done, NITEM * l + i)
                        src = prob[:, it["first"] % NPROB, :]
                        for b in range(TT if it["t"] < TT - 1 else 1):
                            last = pe.transpose(pair[2][:, b * P:(b + 1) * P], src[:, b * P:(b + 1) * P], con("ident"))
                        last.then_inc(tr_done, 1)
                    if n - LAG_V in BY_LAST:
                        i = BY_LAST[n - LAG_V]
                        it = ITEMS[i]
                        pe.wait_ge(pt_done, NITEM * l + i + 1)
                        if it["hh"] == 0 and it["unit"] > 0:
                            pe.wait_ge(o_evac, NUNIT * l + it["unit"])
                        out = psum[64 * it["hh"]:64 * it["hh"] + 64, 6, 0:P]
                        vs = slice(it["vcol"], it["vcol"] + 64)
                        pt = probT[:, i % 2, :]
                        if it["t"] < TT - 1:
                            for b in range(TT):
                                last = pe.matmul(out, vN[:, b, vs] if b < TT - 1 else vc[:, vs],
                                                 pt[:, b * P:(b + 1) * P], start=(b == 0), stop=(b == TT - 1))
                        else:
                            last = pe.matmul(out, vN[:, TT - 1, vs], pt[:, 0:P], start=True, stop=True)
                        last.then_inc(pv_done, 1)
                for b in range(2):
                    pe.wait_ge(b_sq, 2 * l + b + 1)
                    wide(pair[b], lambda k: con("pairsum"), lambda k: sq[:, b, :], 1).then_inc(bn_mm, 1)

            def out_projection(l):
                for c in range(KC):
                    if c >= 2:
                        pe.wait_ge(wout_added, KC * l + c - 1)
                    wide3(pair[OPAIR[c % 2]], take(SPLIT["wout", l, c]), oHL, OCHUNKS, None if c else olow_done,
                          KC * l).then_inc(used, 1)

            def queries(l):
                for s in range(HC + 1):
                    if s < HC:
                        if s >= 2:
                            pe.wait_ge(proj_evac, PROJ * l + NWIN + s - 1)
                        wide3(pair[s % 2], take(SPLIT["wq", l, s]), hHL, ready=None if s else hlow_done,
                              count=KC * (2 * l + 1)).then_inc(used, 1)
                    if s >= 1:
                        r = s - 1
                        if r == 0:
                            pe.wait_ge(keys_in, 16 * (l + 1))
                        pe.wait_ge(proj_evac, PROJ * l + NWIN + r + 1)
                        if r >= 2:
                            pe.wait_ge(scores_in, HC * l + r - 1)
                        for t in range(TT):
                            last = pe.matmul(pair[2 + r % 2][:, t * P:(t + 1) * P], qTb[:, r % 2, t * P:(t + 1) * P],
                                             keys[:, r, :], start=True, stop=True)
                        last.then_inc(keyscore, 1)

            def hidden_pass(l):
                b0 = SPLIT["ex", l, 0]
                base = NU * l

                def u_block(i, k):
                    pe.wait_ge(split_done, i * RING + (b0 + k + 1))
                    if not isinstance(i, int) or i * RING + k >= 2:
                        pe.wait_ge(gelu_done, i * RING + (base + k - 1))
                    wide3(pair[k % 2], split[:, (b0 + k) % RING], hHL).then_inc(used, 1)

                for t in range(TT):
                    tile = TT * l + t
                    for k in range(UA):
                        u_block(6 * t + k // RING, k % RING)
                    pe.wait_ge(route_ready, tile + 1)
                    if t == 0:
                        pe.wait_ge(scores_in, HC * (l + 1))
                    else:
                        pe.wait_ge(g_evac[0], GTURNS * tile + 1)
                    for r in range(3):
                        last = pe.transpose(psum[:, 4, r * P:(r + 1) * P], route[:, r, :], con("ident"))
                    last.then_inc(route_tr, 1)
                    pe.wait_ge(route_in, tile + 1)
                    with pe.Fori(0, 2) as i:
                        for s4 in range(GTURNS // 2):
                            u_block(i + (6 * t + 4), s4)
                            for q in range(GB):
                                turn = i * (GTURNS // 2) + (GTURNS * tile + s4)
                                pe.wait_ge(onehot, turn * GB + (q + 1))
                                pe.wait_ge(g_evac[q], turn + 1)
                                for k in range(4):
                                    s = 4 * q + k
                                    last = pe.matmul(psum[:, 4 + q, k * P:(k + 1) * P], oneh1[:, s, :],
                                                     oneh2[:, s, :], start=True, stop=True)
                                last.then_inc(g_mm[q], 1)
                for k in range(GJ):
                    u_block((NU - GJ) // RING + k // RING, k % RING)

            def output_pass(l):
                b0 = SPLIT["ex", l, NU]
                base = NGROUP * KC * l

                def v_group(g, b):
                    pe.wait_ge(hid_ready, g * 2 + (2 * NGROUP * l + 2))
                    for c in range(KC):
                        pe.wait_ge(split_done, g * GJ + (b0 + c + 1))
                        if not isinstance(g, int) or g * KC + c >= 2:
                            pe.wait_ge(y_added, g * KC + (base + c - 1))
                        wide3(pair[2 + c % 2], split[:, (b0 + c) % RING], hidHL[b]).then_inc(used, 1)

                for q in range(GB):
                    pe.wait_ge(g_evac[q], GTURNS * TT * (l + 1) + 1)
                v_group(0, 0)
                with pe.Fori(0, (NGROUP - 2) // 2) as i:
                    v_group(i * 2 + 1, 1)
                    v_group(i * 2 + 2, 0)
                v_group(NGROUP - 1, 1)

            for q in range(GB):
                pe.sem_inc(g_mm[q], 1)
            pe.wait_ge(inputs_in, 16 * N_INPUTS)
            pe.wait_ge(c_ready, 1)
            for m in range(FIRST_MOD):
                mod_block(0, m)
            for l in range(L):
                norm(2 * l)
                project(l)
                attention(l)
                out_projection(l)
                norm(2 * l + 1)
                queries(l)
                hidden_pass(l)
                output_pass(l)
            norm(2 * L)

        @block.scalar
        def _(act):
            act.wait_ge(inputs_in, 16 * N_INPUTS)
            act.activation(cexp[:], cT[:], ACT.Exp, scale=-1.0).then_inc(silu_exp, 1)
            act.wait_ge(lam_sum, 1)
            act.activation(lsum[:], lsum[:], ACT.Exp).then_inc(lam_exp, 1)

            def high(b):
                act.wait_ge(scale_done, b + 1)
                if b >= RING:
                    act.wait_ge(used, b - RING + 1)
                n = BLOCK[SPLIT_KEYS[b]]
                act.activation(split[:, b % RING, 0], ring[:, n % RING], ACT.Copy,
                               scale=bscale[:, b % RING:b % RING + 1]).then_inc(high_done, 1)

            def high_at(b0, n0, off, k):
                act.wait_ge(scale_done, off + (b0 + k + 1))
                act.wait_ge(used, off + (b0 + k - RING + 1))
                act.activation(split[:, (b0 + k) % RING, 0], ring[:, (n0 + k) % RING], ACT.Copy,
                               scale=bscale[:, (b0 + k) % RING:(b0 + k) % RING + 1]).then_inc(high_done, 1)

            def slot(b):
                if ahead(b + 2, segment(b)):
                    high(b + 2)

            def norm(ni):
                if ni % 2 == 1:
                    act.wait_ge(wout_added, KC * (ni // 2 + 1))
                elif ni == 0:
                    act.wait_ge(residual_in, 16)
                else:
                    act.wait_ge(y_added, NGROUP * KC * (ni // 2))
                for c in range(KC):
                    if c >= 2:
                        act.wait_ge(sum_step, KC * ni + c - 1)
                    act.activation(sq[:, c % 2, :], xT[:, c, :], ACT.Square).then_inc(sq_ready, 1)
                root(*((ni // 2, 0) if ni % 2 == 0 else (ni // 2, 7)))
                if ni < 2 * L:
                    for c in range(KC):
                        act.wait_ge(xhigh_in, KC * ni + c + 1)
                        act.activation(hHL[:, 0, c, :], y32[:, c, :], ACT.Copy).then_inc(xhigh_done, 1)

            def root(l, i):
                act.wait_ge(var_ready, roots(l, i))
                act.activation(var, var, ACT.Sqrt).then_inc(sd_ready, 1)

            def project(l):
                for i in range(NWIN):
                    b = SPLIT["win", l, i]
                    slot(b)
                    act.wait_ge(used, b + 1)
                    act.wait_ge(descale_done, NDESC * l + i + 1)
                    scale = descale[:, b % RING:b % RING + 1]
                    src = pair[i % 2][:, 0:TOK]
                    if i < NQK:
                        act.activation(qk[:, i, :], src, ACT.Copy, scale=scale).then_inc(proj_evac, 1)
                    else:
                        m = i - NQK
                        act.activation(vN[:, :, m * P:(m + 1) * P], src.rearrange("p (t d) -> p t d", t=TT),
                                       ACT.Copy, scale=scale).then_inc(proj_evac, 1)
                    if 3 <= i < 7:
                        r = i - 3
                        act.wait_ge(proj_evac, PROJ * l + r + 1)
                        if r >= 2:
                            act.wait_ge(post_mm, POSTS * l + r - 1)
                        act.activation(sq[:, r % 2, :], qk[:, r, :], ACT.Square).then_inc(c_sq, 1)
                    if 5 <= i < 9:
                        root(l, 1 + i - 5)

            def attention(l):
                for n in range(NMAP + LAG_V):
                    if n < NMAP:
                        m = MAPS[n]
                        w = TOK if m["t"] < TT - 1 else NCTX
                        act.wait_ge(max_done, NMAP * l + n + 1)
                        if n >= NPROB:
                            act.wait_ge(tr_done, NITEM * l + MAPS[n - NPROB]["item"] + 1)
                        act.activation(prob[:, n % NPROB, 0:w], pair[n % 2][:, 0:w], ACT.Exp,
                                       bias=stat[:, 0, n % NPROB:n % NPROB + 1],
                                       accum_out=stat[:, 1, n % NPROB:n % NPROB + 1]).then_inc(exp_done, 1)
                    if n - LAG_T in BY_LAST:
                        i = BY_LAST[n - LAG_T]
                        w = TOK if ITEMS[i]["t"] < TT - 1 else NCTX
                        act.wait_ge(tr_done, NITEM * l + i + 1)
                        if i >= 2:
                            act.wait_ge(pv_done, NITEM * l + i - 1)
                        act.activation(probT[:, i % 2, 0:w], pair[2][:, 0:w], ACT.Copy).then_inc(pt_done, 1)
                    if n - LAG_V in UNIT_BY_LAST:
                        u = UNIT_BY_LAST[n - LAG_V]
                        act.wait_ge(pv_done, NITEM * l + UNITS[u]["last"] + 1)
                        act.activation(oT[:, UNITS[u]["chunk"], UNITS[u]["t"] * P:(UNITS[u]["t"] + 1) * P],
                                       psum[:, 6, 0:P], ACT.Copy).then_inc(o_evac, 1)
                act.wait_ge(o_evac, NUNIT * (l + 1))
                for b in range(2):
                    act.activation(sq[:, b, :], oT[:, 3 + b, :], ACT.Square).then_inc(b_sq, 1)
                b = SPLIT["wout", l, 0]
                high(b)
                high(b + 1)
                act.wait_ge(oscale_done, l + 1)
                for n, c in enumerate(OCHUNKS):
                    if n == 2:
                        for b in range(2):
                            root(l, 5 + b)
                    if c in (3, 4):
                        act.wait_ge(bn_fin, 2 * l + c - 2)
                    act.activation(oHL[:, 0, c, :], oT[:, c, :], ACT.Copy, scale=vscale[:]).then_inc(ohigh_done, 1)

            def out_projection(l):
                for c in range(KC):
                    slot(SPLIT["wout", l, c])

            def queries(l):
                act.wait_ge(kv_stored, 16 * 4 * (l + 1))
                for s in range(HC + 1):
                    if s < HC:
                        b = SPLIT["wq", l, s]
                        slot(b)
                        act.wait_ge(used, b + 1)
                        act.wait_ge(descale_done, NDESC * l + NWIN + s + 1)
                        if s >= 2:
                            act.wait_ge(keyscore, HC * l + s - 1)
                        act.activation(qTb[:, s % 2, :], pair[s % 2][:, 0:TOK], ACT.Copy,
                                       scale=descale[:, b % RING:b % RING + 1]).then_inc(proj_evac, 1)
                    if s >= 1:
                        r = s - 1
                        act.wait_ge(keyscore, HC * l + r + 1)
                        act.activation(scores[:, :, r, :],
                                       pair[2 + r % 2][:, 0:TOK].rearrange("p (t d) -> p t d", t=TT),
                                       ACT.Copy).then_inc(scores_in, 1)

            def hidden_pass(l):
                n0, b0 = BLOCK["ex", l, 0], SPLIT["ex", l, 0]

                def gelu(i, k):
                    high_at(b0, n0, i * RING, k + 2)
                    act.wait_ge(used, i * RING + (b0 + k + 1))
                    act.wait_ge(descale_done, i * RING + (NDESC * l + NWIN + HC + k + 1))
                    if not isinstance(i, int) or 2 * NGROUP * l + i > 0:
                        act.wait_ge(hid_out[k], i * 16 + 32 * NGROUP * l)
                    act.activation(xT[:, k, :], pair[k % 2][:, 0:TOK], ACT.Gelu_apprx_tanh,
                                   scale=descale[:, (b0 + k) % RING:(b0 + k) % RING + 1]).then_inc(gelu_done, 1)

                act.wait_ge(x_out, 16 * (l + 1))
                for t in range(TT):
                    tile = TT * l + t
                    for k in range(UA):
                        if k == EXP_AFTER:
                            act.wait_ge(sub_ready, tile + 1)
                            act.activation(sel, sel, ACT.Exp).then_inc(gexp_ready, 1)
                        gelu(6 * t + k // RING, k % RING)
                    act.wait_ge(route_tr, tile + 1)
                    act.activation(routeT, psum[:, 4, 0:3 * P].rearrange("p (r t) -> p r t", r=3),
                                   ACT.Copy).then_inc(route_in, 1)
                    if tile > 0:
                        act.wait_ge(g_stored, 16 * tile)
                    with act.Fori(0, 2) as i:
                        for s4 in range(GTURNS // 2):
                            gelu(i + (6 * t + 4), s4)
                            for q in range(GB):
                                turn = i * (GTURNS // 2) + (GTURNS * tile + s4)
                                act.wait_ge(g_mm[q], turn + 2)
                                dst = gst[:, :, bass.ds(i * (P // 2) + (s4 * GTOK + 4 * q), 4)]
                                act.activation(dst, psum[:, 4 + q, :].rearrange("p (t j) -> p j t", t=4),
                                               ACT.Copy).then_inc(g_evac[q], 1)
                    for q in range(GB):
                        act.wait_ge(g_evac[q], GTURNS * (tile + 1) + 1)
                    act.dma_start(gdram.rearrange("j i t -> i j t")[:, :, t * P:(t + 1) * P], gst).then_inc(g_stored, 16)
                for k in range(GJ):
                    gelu((NU - GJ) // RING + k // RING, k % RING)

            def output_pass(l):
                n0, b0 = BLOCK["ex", l, NU], SPLIT["ex", l, NU]

                def hidden_high(g, b, half):
                    if half == 0:
                        act.wait_ge(hscale_done, g + (NGROUP * l + 1))
                    act.activation(hidHL[b][:, 0, 4 * half:4 * half + 4, :], hid[b][:, 4 * half:4 * half + 4, :],
                                   ACT.Copy, scale=hscale[:, b:b + 1]).then_inc(hhigh_done, 1)

                def step(g, b):
                    for c in range(KC):
                        high_at(b0, n0, g * GJ, c + 2)
                        if c in (4, 5):
                            hidden_high(g + 1, 1 - b, c - 4)

                hidden_high(0, 0, 0)
                hidden_high(0, 0, 1)
                step(0, 0)
                with act.Fori(0, (NGROUP - 2) // 2) as i:
                    step(i * 2 + 1, 1)
                    step(i * 2 + 2, 0)
                for c in range(KC):
                    slot(b0 + (NGROUP - 1) * GJ + c)

            for q in range(GB):
                act.sem_inc(g_evac[q], 1)
            high(0)
            high(1)
            for l in range(L):
                norm(2 * l)
                project(l)
                attention(l)
                out_projection(l)
                norm(2 * l + 1)
                queries(l)
                hidden_pass(l)
                output_pass(l)
            norm(2 * L)

        @block.vector
        def _(dve):
            links = [0]

            def link(ins):
                links[0] += 1
                ins.then_inc(dve_chain, 1)
                dve.wait_ge(dve_chain, links[0])

            dve.wait_ge(silu_exp, 1)
            link(dve.tensor_scalar(cexp[:], cexp[:], 1.0, None, ALU.add))
            link(dve.reciprocal(cexp[:], cexp[:]))
            dve.tensor_tensor(cT[:], cT[:], cexp[:], ALU.mult).then_inc(c_ready, 1)
            link(dve.tensor_tensor(lprod[:], lam[:, :, 0:4:2, :], lam[:, :, 1:4:2, :], ALU.mult))
            dve.tensor_reduce(lsum[:], lprod[:], AX_X, ALU.add).then_inc(lam_sum, 1)
            dve.wait_ge(lam_exp, 1)
            link(dve.tensor_tensor(nlam[:], lsum[:, :, 1], lsum[:, :, 0], ALU.subtract))
            for l in range(L):
                init = 0.8 - 0.6 * math.exp(-0.3 * l)
                dve.tensor_scalar(nlam[:, l:l + 1], nlam[:, l:l + 1], -init, None, ALU.add).then_inc(lam_ready, 1)
                dve.tensor_scalar(col("qkgain", 2 * l), col("qkgain", 2 * l), 0.125, None, ALU.mult)
                link(dve.tensor_scalar(col("subln", l), col("subln", l), 1.0 - init, None, ALU.mult))

            def power(pow_, scale, src):
                link(dve.tensor_scalar(pow_.bitcast(U32), src.bitcast(U32), EXPONENT, None, ALU.bitwise_and))
                return dve.tensor_scalar(scale.bitcast(U32), pow_.bitcast(U32), -1.0, float((254 + TOP) << 23),
                                         ALU.mult, ALU.add)

            def tick(nb, turns, k, has=lambda j: True):
                off = turns * RING

                def one(j):
                    return slice(j % RING, j % RING + 1)

                if has(k - 2):
                    j = k - 2
                    dve.wait_ge(high_done, off + (j + 1))
                    sp_ = split[:, j % RING].rearrange("p s c m -> p s (c m)")
                    dve.scalar_tensor_tensor(sp_[:, 1, :], ring[:, (j + nb) % RING].rearrange("p c m -> p (c m)"),
                                             bscale[:, one(j)], sp_[:, 0, :], ALU.mult,
                                             ALU.subtract).then_inc(split_done, 1)
                if has(k - 1):
                    j = k - 1
                    dve.wait_ge(ball_done, off + (j + 1))
                    dve.tensor_scalar(bpow[:, one(j)].bitcast(U32), ball[:, one(j)].bitcast(U32), EXPONENT, None,
                                      ALU.bitwise_and).then_inc(bpow_done, 1)
                if has(k):
                    dve.wait_ge(landed[(k + nb) % RING], turns * 16 + 16 * ((k + nb) // RING + 1))
                    dve.tensor_reduce(bmax[:, one(k)], ring[:, (k + nb) % RING].rearrange("p c m -> p (c m)"),
                                      AX_X, ALU.max, apply_absolute_value=True).then_inc(bmax_done, 1)
                if has(k - 1):
                    j = k - 1
                    dve.wait_ge(bpow_done, off + (j + 1))
                    dve.tensor_scalar(bscale[:, one(j)].bitcast(U32), bpow[:, one(j)].bitcast(U32), -1.0,
                                      float((254 + TOP) << 23), ALU.mult, ALU.add).then_inc(scale_done, 1)

            def tick_at(b):
                seg = segment(b)
                k = b + 4
                nb = BLOCK[SPLIT_KEYS[min(k, seg[1])]] - min(k, seg[1])
                tick(nb, 0, k, lambda j: ahead(j, seg))

            def prologue(seg):
                nb = BLOCK[SPLIT_KEYS[seg[0]]] - seg[0]
                for k in range(seg[0], seg[0] + 4):
                    tick(nb, 0, k, lambda j: ahead(j, seg))

            def descales(b, const_=1.0):
                dve.tensor_scalar(descale[:, b % RING:b % RING + 1], bpow[:, b % RING:b % RING + 1], xinv[:],
                                  const_ * 2.0 ** -TOP, ALU.mult, ALU.mult).then_inc(descale_done, 1)

            def modulation(l, lo, hi_, after):
                dve.wait_ge(mod_used, after + 1)
                b = cols[:, FO["bmod"] + NMOD * l + lo:FO["bmod"] + NMOD * l + hi_]
                link(dve.tensor_tensor(modT[:, l, lo:hi_, :], modps[:, l, lo:hi_, :],
                                       b.unsqueeze(2).to_broadcast([P, hi_ - lo, 2]), ALU.add))
                for half in range(2):
                    s = KC * (3 * half + 1)
                    if lo <= s < hi_:
                        gcol = FO["gain"] + KC * (2 * l + half)
                        link(dve.scalar_tensor_tensor(modT[:, l, s:s + KC, :], modT[:, l, s:s + KC, :], 1.0,
                                                      cols[:, gcol:gcol + KC].unsqueeze(2).to_broadcast([P, KC, 2]),
                                                      ALU.add, ALU.mult))

            def root(l, i, ps, n):
                dve.tensor_scalar(var, ps[:, 0:TOK], 1.0 / n, EPS, ALU.mult, ALU.add).then_inc(var_ready, 1)
                dve.wait_ge(sd_ready, roots(l, i))
                link(dve.reciprocal(rs, var))

            def norm(ni):
                l, half = ni // 2, ni % 2
                if ni < 2 * L:
                    m = 3 * KC * half
                    dve.tensor_reduce(xstat[:, 0:1], modT[:, l, m + KC:m + 2 * KC, :].rearrange("p c s -> p (c s)"),
                                      AX_X, ALU.max, apply_absolute_value=True)
                    link(dve.tensor_reduce(xstat[:, 1:2], modT[:, l, m:m + KC, :].rearrange("p c s -> p (c s)"),
                                           AX_X, ALU.max, apply_absolute_value=True))
                    spread(dve.scalar_tensor_tensor(xstat[:, 2:3], xstat[:, 0:1], float(D) ** 0.5, xstat[:, 1:2],
                                                    ALU.mult, ALU.add))
                    link(power(xpow[:], xscale[:], xall[:]))
                    dve.tensor_scalar(xinv[:], xpow[:], 2.0 ** -TOP, None, ALU.mult)
                    dve.tensor_scalar(affine[:, 0], modT[:, l, m + KC:m + 2 * KC, :], xscale[:], None, ALU.mult)
                    link(dve.tensor_scalar(affine[:, 1], modT[:, l, m:m + KC, :], xscale[:], None, ALU.mult))
                dve.wait_ge(sum_step, KC * (ni + 1))
                root(l, 7 if half else 0, pair[0], D)
                if ni == 2 * L:
                    for c in range(KC):
                        last = dve.scalar_tensor_tensor(hT[:, c, :], xT[:, c, :], col("fgain", c), rs,
                                                        ALU.mult, ALU.mult)
                    last.then_inc(y_ready, 1)
                    return
                for c in range(KC + 1):
                    if c < KC:
                        link(dve.tensor_tensor(y32[:, c, :], xT[:, c, :], rs, ALU.mult))
                        for s, (lo, hi_) in enumerate(((0, NLAT), (NLAT, TOK))):
                            last = dve.tensor_scalar(y32[:, c, lo:hi_], y32[:, c, lo:hi_], affine[:, 0, c, s:s + 1],
                                                     affine[:, 1, c, s:s + 1], ALU.mult, ALU.add)
                        last.then_inc(xhigh_in, 1)
                    if c:
                        dve.wait_ge(xhigh_done, KC * ni + c)
                        last = dve.tensor_tensor(hHL[:, 1, c - 1, :], y32[:, c - 1, :], hHL[:, 0, c - 1, :],
                                                 ALU.subtract).then_inc(hlow_done, 1)

            spreads = [0]

            def spread(ins):
                spreads[0] += 1
                ins.then_inc(xmax_done, 1)
                dve.wait_ge(xall_done, spreads[0])

            def project(l):
                for i in range(NWIN):
                    descales(SPLIT["win", l, i], B_SCALE if BQ <= i < BK else 0.125 if AQ <= i < AK else 1.0)
                    tick_at(SPLIT["win", l, i])
                    if i >= 5:
                        posts(l, (i - 5,) if i < 17 else ())

            def posts(l, ps):
                for p in ps:
                    dve.wait_ge(post_mm, POSTS * l + p + 1)
                    if p < 4:
                        root(l, 1 + p, pair[2], 64)
                        dve.scalar_tensor_tensor(qk[:, p, :], qk[:, p, :], col("qkgain", 2 * l + (p == 3)), rs,
                                                 ALU.mult, ALU.mult).then_inc(post_fin, 1)
                    else:
                        ch = p - 4
                        kind = "C" if ch < BQ else "B"
                        if p == 4:
                            dve.wait_ge(layer_in, 16 * 3 * (l + 1))
                        x = qk[:, ch, 0:NLAT]
                        dve.tensor_tensor(var[:, 0:NLAT], pair[2][:, 0:NLAT], tab("sin" + kind), ALU.mult)
                        link(dve.tensor_tensor(x, x, tab("cos" + kind), ALU.mult))
                        dve.tensor_tensor(x, x, var[:, 0:NLAT], ALU.add).then_inc(post_fin, 1)

            def attention(l):
                dve.wait_ge(proj_evac, PROJ * l + NWIN)
                dve.tensor_reduce(xstat[:, 0:1], vN.rearrange("p t v -> p (t v)"), AX_X, ALU.max,
                                  apply_absolute_value=True)
                dve.tensor_reduce(xstat[:, 1:2], vc, AX_X, ALU.max, apply_absolute_value=True)
                link(dve.tensor_scalar(xstat[:, 3:4], col("subln", l), 8.0, None, ALU.mult))
                dve.tensor_reduce(xstat[:, 4:5], xstat[:, 3:4], AX_X, ALU.max, apply_absolute_value=True)
                link(dve.tensor_tensor(xstat[:, 5:6], xstat[:, 0:1], xstat[:, 1:2], ALU.max))
                link(dve.tensor_copy(xstat[:, 6:7], xstat[:, 4:5]))
                spread(dve.tensor_tensor(xstat[:, 2:3], xstat[:, 5:6], xstat[:, 6:7], ALU.max))
                link(power(vpow[:], vscale[:], xall[:]))
                dve.tensor_scalar(vinv[:], vpow[:], 2.0 ** (-2 * TOP), None, ALU.mult).then_inc(oscale_done, 1)
                dve.wait_ge(bias_ready, 6 * (l + 1))
                for n in range(NMAP + 2):
                    if n < NMAP:
                        m = MAPS[n]
                        ps = pair[n % 2]
                        lat = m["t"] < TT - 1
                        dve.wait_ge(score_done, NMAP * l + n + 1)
                        if m["kind"] == "A" and lat:
                            r0 = 6 - 2 * m["t"]
                            b = bias[:, m["head"], r0:r0 + ROWS, :].rearrange("p r c -> p (r c)")
                            link(dve.tensor_tensor(ps[:, 0:NLAT], ps[:, 0:NLAT], b, ALU.add))
                        dve.tensor_reduce(stat[:, 0, n % NPROB:n % NPROB + 1], ps[:, 0:TOK if lat else NCTX], AX_X, ALU.max,
                                          negate=True).then_inc(max_done, 1)
                    if 1 <= n <= NMAP:
                        s = (n - 1) % NPROB
                        dve.wait_ge(exp_done, NMAP * l + n)
                        dve.reciprocal(stat[:, 2, s:s + 1], stat[:, 1, s:s + 1]).then_inc(rinv_done, 1)
                    if n - 2 in BY_LAST and ITEMS[BY_LAST[n - 2]]["kind"] == "B":
                        it = ITEMS[BY_LAST[n - 2]]
                        w = TOK if it["t"] < TT - 1 else NCTX
                        s0, s1 = it["first"] % NPROB, it["last"] % NPROB
                        dve.wait_ge(scaled, NSCALED * l + SCALED[n - 2] + 1)
                        dve.scalar_tensor_tensor(prob[:, s0, 0:w], prob[:, s0, 0:w], stat[:, 2, s0:s0 + 1],
                                                 prob[:, s1, 0:w], ALU.mult, ALU.add).then_inc(mixed, 1)
                prologue(segment(SPLIT["wout", l, 0]))
                after = MODS["mod", *MOD_IN[l][-1]]
                modulation(l, FIRST_MOD, NMOD, after)
                if l + 1 < L:
                    modulation(l + 1, 0, FIRST_MOD, after)
                for n, c in enumerate(OCHUNKS):
                    if n == 2:
                        for b in range(2):
                            dve.wait_ge(bn_mm, 2 * l + b + 1)
                            root(l, 5 + b, pair[b], 64)
                            dve.scalar_tensor_tensor(oT[:, 3 + b, :], oT[:, 3 + b, :], col("subln", l), rs,
                                                     ALU.mult, ALU.mult).then_inc(bn_fin, 1)
                    dve.wait_ge(ohigh_done, KC * l + n + 1)
                    dve.scalar_tensor_tensor(oHL[:, 1, c, :], oT[:, c, :], vscale[:], oHL[:, 0, c, :],
                                             ALU.mult, ALU.subtract).then_inc(olow_done, 1)

            def gate_scale(c, l, m, b, inv):
                return dve.tensor_scalar(gatecol[:, c % 2], modT[:, l, m + c, :], bpow[:, b % RING:b % RING + 1], inv,
                                         ALU.mult, ALU.mult).then_inc(gate_set, 1)

            def residual_add(ps, c):
                for s, (lo, hi_) in enumerate(((0, NLAT), (NLAT, TOK))):
                    last = dve.scalar_tensor_tensor(xT[:, c, lo:hi_], ps[:, lo:hi_], gatecol[:, c % 2, s:s + 1],
                                                    xT[:, c, lo:hi_], ALU.mult, ALU.add)
                return last

            def out_projection(l):
                for c in range(KC):
                    b = SPLIT["wout", l, c]
                    tick_at(b)
                    gate_scale(c, l, 2 * KC, b, vinv[:])
                    dve.wait_ge(gate_set, NRES * l + c + 1)
                    dve.wait_ge(used, b + 1)
                    residual_add(pair[OPAIR[c % 2]], c).then_inc(wout_added, 1)

            def queries(l):
                for s in range(HC):
                    descales(SPLIT["wq", l, s])
                    tick_at(SPLIT["wq", l, s])

            def u_tick(l, i, k):
                b0 = SPLIT["ex", l, 0]
                tick(BLOCK["ex", l, 0] - b0, i, b0 + k + 4)

            def u_slot(l, i, k):
                descales(SPLIT["ex", l, 0] + k)
                u_tick(l, i, k)

            def top16(src, spare, vals, idx, n, turn):
                for r in range(n):
                    last = dve.max(vals[r][:, 0:8], src[r])
                link(last)
                turn()
                for r in range(n):
                    dve.max_index(idx[r][:, 0:8], vals[r][:, 0:8], src[r])
                    last = dve.match_replace(spare[r], vals[r][:, 0:8], src[r], LOWEST)
                link(last)
                turn()
                for r in range(n):
                    last = dve.max(vals[r][:, 8:16], spare[r])
                link(last)
                turn()
                for r in range(n):
                    last = dve.max_index(idx[r][:, 8:16], vals[r][:, 8:16], spare[r])
                link(last)
                turn()

            def gates(l):
                for t in range(TT):
                    tile = TT * l + t
                    turns = iter(range(UA))

                    def turn():
                        k = next(turns)
                        u_slot(l, 6 * t + k // RING, k % RING)

                    if t == 0:
                        dve.wait_ge(scores_in, HC * (l + 1))
                    else:
                        for q in range(GB):
                            dve.wait_ge(g_mm[q], GTURNS * tile + 1)
                    turn()
                    topr = top.rearrange("p h c k -> p (h c) k")
                    topir = topi.rearrange("p (r k) -> p r k", k=TOPK)
                    altr = alt.rearrange("p (r k) -> p r k", k=P)
                    top16([scores[:, t, r, :] for r in range(HC)], [altr[:, r, :] for r in range(HC)],
                          [topr[:, r, :] for r in range(HC)], [topir[:, r, :] for r in range(HC)], HC, turn)
                    c4 = cand.rearrange("p (h a b) -> p h a b", h=HEADS, a=TOPK)
                    link(dve.tensor_tensor(c4, top[:, :, 0, :].unsqueeze(3).to_broadcast([P, HEADS, TOPK, TOPK]),
                                           top[:, :, 1, :].unsqueeze(2).to_broadcast([P, HEADS, TOPK, TOPK]), ALU.add))
                    dve.tensor_copy(topf.rearrange("p h c k -> p (h c k)"), topi)
                    turn()
                    c2 = cand.rearrange("p (h a) -> p h a", h=HEADS)
                    a2 = alt.rearrange("p (h a) -> p h a", h=HEADS)
                    s2 = sel.rearrange("p (h k) -> p h k", h=HEADS)
                    i2 = seli.rearrange("p (h k) -> p h k", h=HEADS)
                    top16([c2[:, h, :] for h in range(HEADS)], [a2[:, h, :] for h in range(HEADS)],
                          [s2[:, h, :] for h in range(HEADS)], [i2[:, h, :] for h in range(HEADS)], HEADS, turn)
                    turn()
                    dve.tensor_copy(gsum[:, 0:HEADS], s2[:, :, 0])
                    link(dve.tensor_scalar(hi, seli, 4, None, ALU.logical_shift_right))
                    dve.tensor_tensor(s2, s2, gsum[:, 0:HEADS].unsqueeze(2).to_broadcast([P, HEADS, TOPK]),
                                      ALU.subtract).then_inc(sub_ready, 1)
                    turn()
                    link(dve.tensor_scalar(seli, seli, 15, None, ALU.bitwise_and))
                    dve.tensor_copy(route[:, 0, :], hi)
                    link(dve.tensor_copy(route[:, 1, :], seli))
                    turn()
                    for half, buf in ((0, alt), (1, cand)):
                        eq = buf.rearrange("p (s a) -> p s a", a=TOPK)
                        dve.tensor_tensor(eq, route[:, half, :].unsqueeze(2).to_broadcast([P, P, TOPK]),
                                          con("iota16").unsqueeze(1).to_broadcast([P, P, TOPK]), ALU.is_equal)
                    link(dve.tensor_copy(gsum[:, HEADS:], gsum[:, 0:HEADS]))
                    turn()
                    for half, buf in ((0, alt), (1, cand)):
                        eq = buf.rearrange("p (h s a) -> p h s a", h=HEADS, a=TOPK)
                        last = dve.tensor_tensor(eq, eq, topf[:, :, half, :].unsqueeze(2).to_broadcast(
                            [P, HEADS, TOPK, TOPK]), ALU.mult)
                    link(last)
                    turn()
                    for half, buf in ((0, alt), (1, cand)):
                        dve.tensor_reduce(route[:, half, :], buf.rearrange("p (s a) -> p s a", a=TOPK), AX_X, ALU.add)
                    turn()
                    dve.wait_ge(gexp_ready, tile + 1)
                    link(dve.tensor_reduce(gsum[:, 0:HEADS], s2, AX_X, ALU.add))
                    link(dve.reciprocal(gsum[:, 0:HEADS], gsum[:, 0:HEADS]))
                    dve.tensor_tensor(route[:, 2, :].rearrange("p (h k) -> p h k", h=HEADS), s2,
                                      gsum[:, 0:HEADS].unsqueeze(2).to_broadcast([P, HEADS, TOPK]),
                                      ALU.mult).then_inc(route_ready, 1)
                    dve.wait_ge(route_in, tile + 1)

                    with dve.Fori(0, 2) as i:
                        for s4 in range(GTURNS // 2):
                            descales(SPLIT["ex", l, 0] + s4)
                            for q in range(GB):
                                dve.wait_ge(g_mm[q], i * (GTURNS // 2) + (GTURNS * tile + s4 + 1))
                                for k in range(4):
                                    s = 4 * q + k
                                    tok = i * (P // 2) + (s4 * GTOK + s)
                                    dve.tensor_scalar(oneh1[:, s, :], con("iota"), routeT[:, 0, bass.ds(tok, 1)],
                                                      None, ALU.is_equal)
                                    last = dve.tensor_scalar(oneh2[:, s, :], con("iota"),
                                                             routeT[:, 1, bass.ds(tok, 1)],
                                                             routeT[:, 2, bass.ds(tok, 1)], ALU.is_equal, ALU.mult)
                                last.then_inc(onehot, 1)
                            u_tick(l, i + (6 * t + 4), s4)

                for k in range(GJ):
                    u_slot(l, (NU - GJ) // RING + k // RING, k % RING)

            def output_pass(l):
                b0 = SPLIT["ex", l, NU]
                nb = BLOCK["ex", l, NU] - b0

                def after(g, n):
                    dve.wait_ge(group_chain, g * GLINKS + (NGROUP * GLINKS * l + n))

                def gating(g, b, turn, c):
                    if c == 0:
                        dve.wait_ge(g_landed[b], turn * 64 + 64 * (NGROUP // 2 * l + 1))
                    if c < 4:
                        js = slice(2 * c, 2 * c + 2)
                        dve.tensor_tensor(hid[b][:, js, :], hid[b][:, js, :], gate[b][:, js, :],
                                          ALU.mult).then_inc(group_chain, 1)
                        after(g, c + 1)
                        last = dve.tensor_reduce(hmax[:, c:c + 1], hid[b][:, js, :].rearrange("p j t -> p (j t)"),
                                                 AX_X, ALU.max, apply_absolute_value=True)
                        if c == 3:
                            last.then_inc(group_chain, 1)
                            after(g, 5)
                            dve.tensor_reduce(gmax[:], hmax[:], AX_X, ALU.max).then_inc(gmax_done, 1)
                    if c == 4:
                        dve.wait_ge(gall_done, g + (NGROUP * l + 1))
                        dve.tensor_scalar(hpow[:, b:b + 1].bitcast(U32), gall[:].bitcast(U32), EXPONENT, None,
                                          ALU.bitwise_and).then_inc(group_chain, 1)
                        after(g, 6)
                        dve.tensor_scalar(hscale[:, b:b + 1].bitcast(U32), hpow[:, b:b + 1].bitcast(U32), -1.0,
                                          float((254 + TOP) << 23), ALU.mult, ALU.add).then_inc(hscale_done, 1)
                        dve.tensor_scalar(hinv[:, b:b + 1], hpow[:, b:b + 1], 2.0 ** (-2 * TOP), None,
                                          ALU.mult).then_inc(group_chain, 1)
                    if c >= 6:
                        js = slice(4 * (c - 6), 4 * (c - 6) + 4)
                        dve.wait_ge(hhigh_done, g * 2 + (2 * NGROUP * l + c - 5))
                        dve.scalar_tensor_tensor(
                            *[x.rearrange("p j t -> p (j t)") for x in (hidHL[b][:, 1, js, :], hid[b][:, js, :])],
                            hscale[:, b:b + 1], hidHL[b][:, 0, js, :].rearrange("p j t -> p (j t)"),
                            ALU.mult, ALU.subtract).then_inc(hid_ready, 1)

                def step(g, b, turn):
                    for c in range(KC):
                        tick(nb, g * 2, b0 + c + 4)
                        gating(g + 1, 1 - b, turn, c)
                        output(g, b, c)

                def output(g, b, c):
                    if c == 0:
                        after(g, GLINKS)
                    gate_scale(c, l, 5 * KC, b0 + c, hinv[:, b:b + 1])
                    dve.wait_ge(gate_set, g * KC + (NRES * l + KC + c + 1))
                    dve.wait_ge(used, g * KC + (b0 + c + 1))
                    residual_add(pair[2 + c % 2], c).then_inc(y_added, 1)

                for c in range(KC):
                    gating(0, 0, 0, c)
                dve.wait_ge(x_in, 16 * (l + 1))
                step(0, 0, 0)
                with dve.Fori(0, (NGROUP - 2) // 2) as i:
                    step(i * 2 + 1, 1, i + 1)
                    step(i * 2 + 2, 0, i + 1)
                for c in range(KC):
                    tick_at(b0 + (NGROUP - 1) * GJ + c)
                    output(NGROUP - 1, 1, c)

            modulation(0, 0, FIRST_MOD, MODS["mod", 0, FIRST_MOD - 1])
            prologue(SEGMENTS[0])
            for l in range(L):
                norm(2 * l)
                project(l)
                attention(l)
                out_projection(l)
                norm(2 * l + 1)
                queries(l)
                gates(l)
                output_pass(l)
            norm(2 * L)

        @block.gpsimd
        def _(pool):
            def reduce_clamped(dst, src, reduced, count):
                pool.sem_inc(asked, 1)
                pool.partition_all_reduce(dst, src, P, bass.bass_isa.ReduceOp.max).then_inc(reduced, 1)
                pool.wait_ge(reduced, count)
                return pool.tensor_tensor(dst, dst, tiny[:], ALU.add)

            def block_max(b, off=0):
                one = slice(b % RING, b % RING + 1)
                pool.wait_ge(bmax_done, off + (b + 1))
                reduce_clamped(ball[:, one], bmax[:, one], block_reduced, off + (b + 1)).then_inc(ball_done, 1)

            def slot_max(b):
                if ahead(b + 4, segment(b)):
                    block_max(b + 4)

            spreads = [0]

            def spread():
                spreads[0] += 1
                pool.wait_ge(xmax_done, spreads[0])
                reduce_clamped(xall[:], xstat[:, 2:3], x_reduced, spreads[0]).then_inc(xall_done, 1)

            def group_max(l, g):
                pool.wait_ge(gmax_done, g + (NGROUP * l + 1))
                reduce_clamped(gall[:], gmax[:], g_reduced, g + (NGROUP * l + 1)).then_inc(gall_done, 1)

            pool.memset(tiny[:], TINY).then_inc(tiny_set, 1)
            pool.wait_ge(tiny_set, 1)
            pool.wait_ge(inputs_in, 16 * N_INPUTS)
            for l in range(L):
                if l:
                    pool.wait_ge(y_added, NGROUP * KC * l)
                pool.dma_start(table, a["tables"]).then_inc(layer_in, 16)
                pool.dma_start(kc, a["cache_kT"][l]).then_inc(layer_in, 16)
                pool.dma_start(vc, a["cache_v"][l]).then_inc(layer_in, 16)
                for par in range(2):
                    pool.dma_start(bias[64 * par:64 * par + 64],
                                   a["rpb"][l, :, :, 1 - par:1 - par + BROWS, :]).then_inc(bias_in, 16)
                if l == 0:
                    for b in range(4):
                        block_max(b)
                spread()
                for i in range(NWIN):
                    slot_max(SPLIT["win", l, i])
                    h = i - 8
                    if h == 0:
                        pool.wait_ge(bias_in, 16 * 2 * (l + 1))
                    if 0 <= h < 6:
                        pool.tensor_tensor(bias[:, h], bias[:, h], con("mask").unsqueeze(1).to_broadcast(
                            [P, BROWS, 64]), ALU.add).then_inc(bias_ready, 1)
                spread()
                pool.wait_ge(proj_evac, PROJ * l + NWIN)
                pool.wait_ge(post_fin, POSTS * l + 4)
                for j, (ch, n) in enumerate(((CK, 1), (BK, 2), (AK, 3))):
                    pool.dma_start(a["out_kT"][l, :, (0, 1, 3)[j]:(0, 1, 3)[j] + n],
                                   qk[:, ch:ch + n, NLAT:TOK]).then_inc(kv_stored, 16)
                pool.dma_start(a["out_v"][l], vN[:, TT - 1, :]).then_inc(kv_stored, 16)
                pool.wait_ge(lam_ready, L)
                for n in range(NMAP):
                    if n in SCALED:
                        m = MAPS[n]
                        w = TOK if m["t"] < TT - 1 else NCTX
                        s = n % NPROB
                        pool.wait_ge(rinv_done, NMAP * l + n + 1)
                        pool.tensor_scalar(prob[:, s, 0:w], prob[:, s, 0:w], stat[:, 2, s:s + 1],
                                           nlam[:, l:l + 1] if m["kind"] == "B" else 1.0,
                                           ALU.mult, ALU.mult).then_inc(scaled, 1)
                for c in range(4):
                    block_max(SPLIT["wout", l, c])
                for c in range(KC):
                    slot_max(SPLIT["wout", l, c])
                spread()
                pool.wait_ge(kv_stored, 16 * 4 * (l + 1))
                pool.wait_ge(hlow_done, KC * (2 * l + 2))
                pool.dma_start(keys, a["keysT"][l]).then_inc(keys_in, 16)
                b0 = SPLIT["wq", l, 4]
                with pool.Fori(0, (HC + NU) // RING) as i:
                    for k in range(RING):
                        block_max(b0 + k, i * RING)
                group_max(l, 0)
                b0 = SPLIT["ex", l, NU] + 4
                with pool.Fori(0, NGROUP - 1) as g:
                    for c in range(KC):
                        block_max(b0 + c, g * KC)
                        if c == 3:
                            group_max(l, g + 1)
                for c in range(KC):
                    slot_max(SPLIT["ex", l, NU + (NGROUP - 1) * GJ + c])


def constants():
    p = np.arange(P)
    c = {}
    c["ident"] = np.eye(P)
    c["ones"] = np.ones((P, P))
    c["pairsum"] = (p[:, None] // 64 == p[None, :] // 64)
    for name, n in (("rotB", 8), ("rotC", 16)):
        m = np.zeros((P, P))
        for d in range(P):
            if d % (2 * n) < n:
                m[d + n, d] = -1.0
            else:
                m[d - n, d] = 1.0
        c[name] = m
    c["iota"] = np.tile(np.arange(P), (P, 1))
    c["iota16"] = np.tile(np.arange(16), (P, 1))
    qc = p[:, None] % GRID_W
    kcol = np.arange(GRID_W)[None, :]
    lo = np.clip(qc - 8, 0, GRID_W - 16)
    c["mask"] = np.where((kcol >= lo) & (kcol < lo + 16), 0.0, NEG)
    tok = np.arange(NLAT)
    t = {}
    for name, dim in (("C", 64), ("B", 32)):
        q = dim // 4
        d = p % dim
        inv = (np.float32(10000.0) ** (-(np.arange(q, dtype=np.float32)) / np.float32(q))).astype(np.float32)
        pos = np.where((d // (dim // 2) == 0)[:, None], (tok // GRID_W)[None, :], (tok % GRID_W)[None, :])
        ang = pos.astype(np.float32) * inv[d % q][:, None]
        t["cos" + name] = np.cos(ang)
        t["sin" + name] = np.sin(ang)
    cat = lambda parts, src: np.concatenate([src[n] for n, _ in parts], 1).astype(np.float32)
    return cat(CONSTS, c), cat(TABLES, t)


def blocks(w):
    K, M = w.shape
    return w.reshape(K // P, P, M // P, P).transpose(2, 1, 0, 3)


def chunked(v):
    v = v.reshape(*v.shape[:-1], -1, P)
    return np.moveaxis(v, -1, 0)


C_PAIRS = [0, 3, 1, 4, 2, 5]


def kernel(x_prompt, x_sample, cache_a_k, cache_a_v, cache_b_k, cache_b_v, cache_c_k, cache_c_v, c, c_ctx,
           w_mod, b_mod, norm_g, w_in, w_out, na_rpb, diff_lambda, diff_subln, gqa_qk_norm, peer_wq,
           peer_keys, peer_u, peer_v, final_g):
    import concourse.bacc as bacc
    from concourse.bass_utils import run_bass_kernel_spmd

    ins = {}
    x = np.concatenate([x_sample.reshape(NLAT, D), x_prompt.reshape(NCTX, D)], 0)
    ins["xT"] = x.T.reshape(KC, P, TOK).transpose(1, 0, 2)
    ins["cT"] = np.stack([c.reshape(KC, P).T, c_ctx.reshape(KC, P).T], 2)
    ins["const"], ins["tables"] = constants()
    ins["cols"] = np.concatenate([
        chunked(b_mod).reshape(P, -1), chunked(norm_g).reshape(P, -1), chunked(final_g).reshape(P, -1),
        np.concatenate([gqa_qk_norm, gqa_qk_norm], -1).reshape(L * 2, P).T,
        np.concatenate([diff_subln, diff_subln], -1).T], 1)
    ins["lam"] = diff_lambda
    ins["w_mod"] = np.stack([blocks(w_mod[l]) for l in range(L)])
    edge = np.cumsum([0, 384, 384, 384, 256, 256, 256, 384, 128, 128])
    part = [np.arange(edge[i], edge[i + 1]) for i in range(9)]
    pairs = np.concatenate([np.arange(64 * h, 64 * h + 64) for h in C_PAIRS])
    order = np.concatenate([part[6][pairs], part[7], part[3], part[4], part[0], part[1], part[2], part[5], part[8]])
    ins["w_in"] = np.stack([blocks(w_in[l][:, order]) for l in range(L)])
    rows = np.concatenate([np.arange(640), 640 + pairs])
    ins["w_out"] = np.stack([blocks(w_out[l][rows]) for l in range(L)])
    ins["w_query"] = np.stack([blocks(peer_wq[l]) for l in range(L)])
    ins["keysT"] = peer_keys.reshape(L, HC, NK, P).transpose(0, 3, 1, 2)
    u = peer_u.reshape(L, P, NGROUP, GJ, KC, P).transpose(0, 2, 3, 5, 4, 1)
    v = peer_v.reshape(L, P, NGROUP, GJ, KC, P).transpose(0, 2, 4, 1, 3, 5)
    ex = np.empty((L, 2 * NGROUP * GJ, P, KC, P), u.dtype)
    seq = [("u", g) for g in range(NGROUP)] + [("v", g) for g in range(NGROUP)]
    for n, (kind, g) in enumerate(seq):
        ex[:, n * GJ:(n + 1) * GJ] = (u if kind == "u" else v)[:, g]
    ins["expert"] = ex
    rpb = np.zeros((L, 6, 15, 127), na_rpb.dtype)
    rpb[..., 63 - 15:63 + 16] = na_rpb
    ins["rpb"] = np.stack([rpb[..., 63 - q:127 - q] for q in range(GRID_W)], 1)
    ck = np.concatenate([cache_c_k.reshape(L, NCTX, P), cache_b_k.reshape(L, NCTX, 2 * P),
                         cache_a_k.reshape(L, NCTX, 3 * P)], 2)
    ins["cache_kT"] = ck.reshape(L, NCTX, 6, P).transpose(0, 3, 2, 1)
    ins["cache_v"] = np.concatenate([cache_a_v.reshape(L, NCTX, -1), cache_b_v.reshape(L, NCTX, -1),
                                     cache_c_v.reshape(L, NCTX, -1)], 2)
    outs = {"out_yT": (P, KC, TOK), "out_kT": (L, P, 6, NCTX), "out_v": (L, NCTX, VW)}

    nc = bacc.Bacc("TRN2", target_bir_lowering=False, num_devices=1)
    arrays, args = {}, {}
    for name, v_ in ins.items():
        arrays[name + "_dram"] = np.ascontiguousarray(v_)
        args[name] = nc.dram_tensor(name + "_dram", v_.shape, F32, kind="ExternalInput").ap()
    for name, shape in outs.items():
        args[name] = nc.dram_tensor(name, shape, F32, kind="ExternalOutput").ap()
    build(nc, args)
    r = run_bass_kernel_spmd(nc, [arrays], core_ids=[0]).results[0]
    y = r["out_yT"].transpose(2, 1, 0).reshape(TOK, D)
    kT = r["out_kT"].transpose(0, 3, 2, 1).reshape(L, NCTX, 6 * P)
    v = r["out_v"]
    return (y[NLAT:].reshape(1, NCTX, D), y[:NLAT].reshape(1, NLAT, D),
            kT[..., 384:].reshape(1, L, NCTX, 6, 64), v[..., 0:384].reshape(1, L, NCTX, 6, 64),
            kT[..., 128:384].reshape(1, L, NCTX, 4, 2, 32), v[..., 384:640].reshape(1, L, NCTX, 4, 64),
            kT[..., 0:128].reshape(1, L, NCTX, 2, 64), v[..., 640:].reshape(1, L, NCTX, 2, 64))
```
